# Optimizing a Trainium2 kernel written in Bass

```python
import jax, jax.numpy as jnp
from jax import lax
import numpy as np

D_MODEL = 1024
BATCH = 1
SEQ = 1024
DEPTH = 1

N_META = 16
HEAD_DIM = 64
CONF_HEADS = 8
SC_HEADS = 8
CONF_W = CONF_HEADS * HEAD_DIM
SC_W = SC_HEADS * HEAD_DIM
MIX_W = CONF_W + SC_W
PROJ_W = 2 * CONF_W + 3 * SC_W
CONF_KERNEL = 31
SC_KERNEL = 3
N_GROUPS = 4
EXPERTS_PER_GROUP = 8
N_EXPERTS = N_GROUPS * EXPERTS_PER_GROUP
TOP_K_EXPERT = 2
D_EXPERT = 512
MOE_BLOCK = 256
EPS = 1e-6

kernel_name = "hymba_conformer_shortconv_hier_moe"

def rms_norm(x, g):
    xf = x.astype(jnp.float32)
    y = xf * lax.rsqrt(jnp.mean(xf * xf, axis=-1, keepdims=True) + EPS)
    return (y * g.astype(jnp.float32)).astype(x.dtype)

def layer_norm(x, g, b):
    xf = x.astype(jnp.float32)
    mu = jnp.mean(xf, axis=-1, keepdims=True)
    xc = xf - mu
    y = xc * lax.rsqrt(jnp.mean(xc * xc, axis=-1, keepdims=True) + EPS)
    return (y * g.astype(jnp.float32) + b.astype(jnp.float32)).astype(x.dtype)

def causal_depthwise_conv(x, w):
    k, c = w.shape
    return lax.conv_general_dilated(
        x, w[:, None, :].astype(x.dtype), window_strides=(1,), padding=[(k - 1, 0)],
        dimension_numbers=("NWC", "WIO", "NWC"), feature_group_count=c)

def hierarchical_route(xf, w_rg, b_rg, w_re, b_re):
    x32 = xf.astype(jnp.float32)
    g_logits = x32 @ w_rg.astype(jnp.float32) + b_rg.astype(jnp.float32)
    g_prob = jax.nn.softmax(g_logits, axis=-1)
    g_top, g_idx = lax.top_k(g_prob, 1)
    e_logits = (x32 @ w_re.astype(jnp.float32) + b_re.astype(jnp.float32)).reshape(
        -1, N_GROUPS, EXPERTS_PER_GROUP)
    e_logits = jnp.take_along_axis(e_logits, g_idx[:, :, None], axis=1)[:, 0]
    e_prob = jax.nn.softmax(e_logits, axis=-1)
    e_top, e_loc = lax.top_k(e_prob, TOP_K_EXPERT)
    e_top = e_top / jnp.sum(e_top, axis=-1, keepdims=True)
    expert_id = g_idx * EXPERTS_PER_GROUP + e_loc
    expert_w = g_top * e_top
    return expert_id.astype(jnp.int32), expert_w

def routed_experts(xf, expert_id, expert_w, w_gate, w_up, w_down):
    n_tok, d = xf.shape
    n_asg = n_tok * TOP_K_EXPERT
    n_blocks = -(-n_asg // MOE_BLOCK) + N_EXPERTS
    flat_e = expert_id.reshape(-1)
    order = jnp.argsort(flat_e)
    sorted_e = flat_e[order]
    counts = jnp.bincount(flat_e, length=N_EXPERTS)
    padded = (counts + MOE_BLOCK - 1) // MOE_BLOCK * MOE_BLOCK
    pad_end = jnp.cumsum(padded)
    pad_start = pad_end - padded
    start = jnp.cumsum(counts) - counts
    dest_sorted = pad_start[sorted_e] + jnp.arange(n_asg, dtype=jnp.int32) - start[sorted_e]
    dest = jnp.zeros((n_asg,), jnp.int32).at[order].set(dest_sorted.astype(jnp.int32))
    src_tok = jnp.arange(n_asg, dtype=jnp.int32) // TOP_K_EXPERT
    row_tok = jnp.full((n_blocks * MOE_BLOCK,), n_tok, jnp.int32).at[dest].set(src_tok)
    block_e = jnp.minimum(
        jnp.searchsorted(pad_end, jnp.arange(n_blocks, dtype=jnp.int32) * MOE_BLOCK, side="right"),
        N_EXPERTS - 1)
    x_pad = jnp.concatenate([xf, jnp.zeros((1, d), xf.dtype)], axis=0)
    x_blocks = x_pad[row_tok].reshape(n_blocks, MOE_BLOCK, d)

    def expert_block(args):
        xb, e = args
        hid = jax.nn.silu(xb @ w_gate[e]) * (xb @ w_up[e])
        return hid @ w_down[e]

    y_blocks = lax.map(expert_block, (x_blocks, block_e))
    y_asg = y_blocks.reshape(-1, d)[dest].reshape(n_tok, TOP_K_EXPERT, d)
    return jnp.einsum("nk,nkd->nd", expert_w.astype(y_asg.dtype), y_asg)

def setup_inputs(seed: int = 0) -> dict:
    key = jax.random.key(seed)
    ks = jax.random.split(key, 20)
    f32 = jnp.float32
    nrm = lambda k, shape, scale: jax.random.normal(k, shape, f32) * scale
    return {
        "x": nrm(ks[0], (BATCH, SEQ, D_MODEL), 1.0),
        "meta_tokens": nrm(ks[1], (N_META, D_MODEL), 1.0),
        "norm_mix_g": 1.0 + nrm(ks[2], (DEPTH, D_MODEL), 0.02),
        "w_in": nrm(ks[3], (DEPTH, D_MODEL, PROJ_W), D_MODEL ** -0.5),
        "conf_dw_w": nrm(ks[4], (DEPTH, CONF_KERNEL, CONF_W), CONF_KERNEL ** -0.5),
        "conf_dw_b": nrm(ks[5], (DEPTH, CONF_W), 0.02),
        "conf_ln_g": 1.0 + nrm(ks[6], (DEPTH, CONF_W), 0.02),
        "conf_ln_b": nrm(ks[7], (DEPTH, CONF_W), 0.02),
        "sc_conv_w": nrm(ks[8], (DEPTH, SC_KERNEL, SC_W), SC_KERNEL ** -0.5),
        "w_out": nrm(ks[9], (DEPTH, MIX_W, D_MODEL), MIX_W ** -0.5),
        "norm_ffn_g": 1.0 + nrm(ks[10], (DEPTH, D_MODEL), 0.02),
        "w_router_group": nrm(ks[11], (DEPTH, D_MODEL, N_GROUPS), D_MODEL ** -0.5),
        "b_router_group": nrm(ks[12], (DEPTH, N_GROUPS), 0.01),
        "w_router_expert": nrm(ks[13], (DEPTH, D_MODEL, N_EXPERTS), D_MODEL ** -0.5),
        "b_router_expert": nrm(ks[14], (DEPTH, N_EXPERTS), 0.01),
        "w_exp_gate": nrm(ks[15], (DEPTH, N_EXPERTS, D_MODEL, D_EXPERT), D_MODEL ** -0.5),
        "w_exp_up": nrm(ks[16], (DEPTH, N_EXPERTS, D_MODEL, D_EXPERT), D_MODEL ** -0.5),
        "w_exp_down": nrm(ks[17], (DEPTH, N_EXPERTS, D_EXPERT, D_MODEL), D_EXPERT ** -0.5),
        "final_norm_g": 1.0 + nrm(ks[18], (D_MODEL,), 0.02),
    }

def reference(x, meta_tokens, norm_mix_g, w_in, conf_dw_w, conf_dw_b, conf_ln_g, conf_ln_b,
              sc_conv_w, w_out, norm_ffn_g, w_router_group, b_router_group, w_router_expert,
              b_router_expert, w_exp_gate, w_exp_up, w_exp_down, final_norm_g):
    bsz = x.shape[0]
    meta = jnp.broadcast_to(meta_tokens.astype(x.dtype)[None], (bsz, N_META, D_MODEL))
    h = jnp.concatenate([meta, x], axis=1)
    t_len = h.shape[1]
    for l in range(DEPTH):
        xn = rms_norm(h, norm_mix_g[l])
        proj = xn @ w_in[l]
        u, gl, sc_b, sc_c, v = jnp.split(
            proj, [CONF_W, 2 * CONF_W, 2 * CONF_W + SC_W, 2 * CONF_W + 2 * SC_W], axis=-1)
        a = u * jax.nn.sigmoid(gl)
        a = causal_depthwise_conv(a, conf_dw_w[l]) + conf_dw_b[l]
        a = jax.nn.silu(layer_norm(a, conf_ln_g[l], conf_ln_b[l]))
        s = sc_b * causal_depthwise_conv(sc_c * v, sc_conv_w[l])
        h = h + jnp.concatenate([a, s], axis=-1) @ w_out[l]
        hn = rms_norm(h, norm_ffn_g[l]).reshape(-1, D_MODEL)
        expert_id, expert_w = hierarchical_route(
            hn, w_router_group[l], b_router_group[l], w_router_expert[l], b_router_expert[l])
        moe = routed_experts(hn, expert_id, expert_w, w_exp_gate[l], w_exp_up[l], w_exp_down[l])
        h = h + moe.reshape(bsz, t_len, D_MODEL)
    out = rms_norm(h, final_norm_g)
    return out[:, N_META:]


_drawn_inputs = setup_inputs


def setup_inputs(seed=0):
    import zlib

    import numpy as np

    out = dict(_drawn_inputs(seed))
    spreads = {}
    factors = {'conf_ln_g': 3.148,
     'conf_ln_b': 3.46,
     'norm_ffn_g': 2.668,
     'b_router_group': 5.206,
     'b_router_expert': 5.513,
     'final_norm_g': 2.913}
    for name, (base, spread) in spreads.items():
        noise = np.random.default_rng([zlib.crc32(name.encode()), seed]).standard_normal(out[name].shape)
        drawn = base * np.exp(spread * noise) if base else spread * noise
        out[name] = __import__('jax').numpy.asarray(drawn.astype(out[name].dtype))
    for name, factor in factors.items():
        out[name] = (out[name] * factor).astype(out[name].dtype)
    return out
```

```python
import concourse.bass as bass
from concourse import mybir
from concourse.alu_op_type import AluOpType as ALU

ACT = mybir.ActivationFunctionType
AX = mybir.AxisListType
F32 = mybir.dt.float32
F32R = mybir.dt.float32r
I32 = mybir.dt.int32
U32 = mybir.dt.uint32

P = 128
D = 1024
KD = D // P
META = 16
SEQ = 1024
NT = SEQ // P
TG = META + SEQ
CW = 512
NJ = CW // P
TAPS, STAPS = 31, 3
PAD = TAPS - 1 - META
ROLES = 5
GL, UU, CC, VV, BB = range(ROLES)
BLK = [(0, 348), (348, 346), (694, 346)]
NCH = TAPS + 3 + STAPS
CB, LG, LB, SW = TAPS, TAPS + 1, TAPS + 2, TAPS + 3
NG, NEG = 4, 8
NE = NG * NEG
NL = NG + NE
F = 512
KF = F // P
GUC, DNC = 8, 4
MAXB = 2 * SEQ // P
SLOTS = 48
EPS = 1e-6
OOB = 4096


class Tally:

    def __init__(self, eng, sem):
        self.eng, self.sem, self.n, self.term = eng, sem, 0, None

    def value(self):
        return self.n if self.term is None else self.term + self.n

    def step(self, ins):
        ins.then_inc(self.sem, 1)
        self.n += 1
        self.eng.wait_ge(self.sem, self.value())

    def loop(self, i, per, first=0):
        self.saved, self.per, self.first = self.n, per, first
        self.term = (i - first) * per if first else i * per

    def end(self, trips):
        assert self.n - self.saved == self.per, (self.n - self.saved, self.per)
        self.n = self.saved + self.per * trips
        self.term = None


def trunk(nc, x, meta, w_in, chan, g_mix, w_out, g_ffn, w_rt, b_rt, w_gate, w_up, w_down, g_fin, out):
    hn_rows = nc.dram_tensor("hn_rows", (SEQ, D), F32).ap()
    y_rows = nc.dram_tensor("y_rows", (2 * SEQ, D), F32).ap()

    R1, R2, R3, R4, ST, SM = 0, 66560, 107520, 140288, 157056, 206208
    base0 = (nc.sbuf_base + 31) // 32 * 32

    def at(name, shape, dt, offset):
        return nc.alloc_sbuf_tensor_at(name, shape, dt, offset=base0 + offset)

    class Bump:
        def __init__(self, start, end):
            self.o, self.end = start, end

        def __call__(self, name, shape, dt=F32):
            n = 4
            for s in shape[1:]:
                n *= s
            t = at(name, shape, dt, self.o)
            self.o += (n + 31) // 32 * 32
            assert self.o <= self.end, (name, self.o, self.end)
            return t

    xn_hi = at("xn_hi", [P, KD, TG], F32R, R1)
    xn_lo = at("xn_lo", [P, KD, TG], F32R, R1 + KD * TG * 4)
    wi_hi = at("wi_hi", [P, ROLES, KD * P], F32R, R2)
    wi_lo = at("wi_lo", [P, ROLES, KD * P], F32R, R2 + ROLES * KD * P * 4)
    mix = at("mix", [P, KD, SEQ], F32, R3)
    r = Bump(R3, R4)
    x_in = r("x_in", [P, 2, D])
    x_sc = r("x_sc", [P, 2, D])
    g_mix_b = r("g_mix_b", [P, D])
    r = Bump(R4, ST)
    a_buf = r("a_buf", [P, PAD + TG])
    cv = r("cv", [P, TG])
    sig = r("sig", [P, TG])
    c_sb = r("c_sb", [P, TG])
    r = Bump(R4, ST)
    sq = r("sq", [P, NJ, 512])
    std = r("std", [P, 512])
    rstd = r("rstd", [P, 512])
    wo_hi = at("wo_hi", [P, KD, D], F32R, R1)
    wo_lo = at("wo_lo", [P, KD, D], F32R, R1 + KD * D * 4)
    r = Bump(R2, R3)
    m_hi = r("m_hi", [P, 2, KD, P], F32R)
    m_lo = r("m_lo", [P, 2, KD, P], F32R)
    x_res = r("x_res", [P, 2, D])
    hn = r("hn", [P, 2, D])
    hn_t = r("hn_t", [P, KD, P])
    g_ffn_b = r("g_ffn_b", [P, D])
    r = Bump(R4, ST)
    tri = r("tri", [P, P])
    ones = r("ones", [P, P])
    iota_r = r("iota_r", [P, P])
    iota_s = r("iota_s", [P, SLOTS])
    part = r("part", [P, 1])
    part1 = r("part1", [P, 1])
    rev = r("rev", [P, NEG])
    thr = r("thr", [P, 7, NE])
    asg_id = r("asg_id", [P, 2, NT])
    a1 = r("a1", [P, NT, NG, NEG])
    a2 = r("a2", [P, NT, NG, NEG])
    a12 = r("a12", [P, NT, NE])
    before = r("before", [P, NT + 1, NE])
    pos = r("pos", [P, NT, NE])
    dest = r("dest", [P, NT, NE])
    prod = r("prod", [P, NT, NE])
    more = r("more", [P, 7, NE])
    r = Bump(R2, R3)
    one_r = r("one_r", [P, 2 * NT, P])
    one_s = r("one_s", [P, 2 * NT, SLOTS])
    val_s = r("val_s", [P, 2 * NT, 2, SLOTS])
    g_sh = r("g_sh", [P, NT, NG])
    g_ex = r("g_ex", [P, NT, NG])
    g_one = r("g_one", [P, NT, NG])
    g_key = r("g_key", [P, NT, NG])
    sel = r("sel", [P, NT, NEG])
    sel2 = r("sel2", [P, NT, NEG])
    key = r("key", [P, NT, NEG])
    o1 = r("o1", [P, NT, NEG])
    o2 = r("o2", [P, NT, NEG])
    vec = r("vec", [P, 12, NT])
    wk = r("wk", [P, 2, NT])
    dd = r("dd", [P, 2, NT])
    dd_i = r("dd_i", [P, 2, NT], I32)
    sl_i = r("sl_i", [P, 2, NT], I32)
    ro_i = r("ro_i", [P, 2, NT], I32)
    sl_f = r("sl_f", [P, 2, NT])
    ro_f = r("ro_f", [P, 2, NT])
    nblk = r("nblk", [P, NE])
    s_end = r("s_end", [P, NE])
    s_beg = r("s_beg", [P, NE])
    junk = r("junk", [P, NE])
    tab = r("tab", [P, 3])
    vm = r("vm", [P, SLOTS])
    inv = r("inv", [P, SLOTS])
    v_i = r("v_i", [P, SLOTS], I32)
    v_f = r("v_f", [P, SLOTS])
    gu_hi = at("gu_hi", [P, GUC, D], F32R, R1)
    gu_lo = at("gu_lo", [P, GUC, D], F32R, R1 + GUC * D * 4)
    dn_hi = at("dn_hi", [P, DNC, D], F32R, R2)
    dn_lo = at("dn_lo", [P, DNC, D], F32R, R2 + DNC * D * 4)
    xt_hi = at("xt_hi", [P, KD, P], F32R, R2 + 2 * DNC * D * 4)
    xt_lo = at("xt_lo", [P, KD, P], F32R, R2 + 2 * DNC * D * 4 + D * 4)
    r = Bump(R4, ST)
    ht_hi = r("ht_hi", [P, KF, P], F32R)
    ht_lo = r("ht_lo", [P, KF, P], F32R)
    x_g = r("x_g", [P, D])
    y_sb = r("y_sb", [P, D])
    hid = r("hid", [P, F])
    sil = r("sil", [P, F])
    r = Bump(R1, R3)
    ys = r("ys", [P, NT, 2, D])
    g_fin_b = r("g_fin_b", [P, D])
    z = r("z", [P, 2, D])
    o_sb = r("o_sb", [P, 2, D])
    f_sq = r("f_sq", [P, D])

    stage = at("stage", [P, GUC + DNC, D], F32, ST)
    r = Bump(SM, SM + 6624)
    ident = r("ident", [P, P])
    ones_cw = r("ones_cw", [P, P])
    chan_sb = r("chan_sb", [P, NJ * NCH])
    logit = r("logit", [P, NT, NL])
    w_rt_sb = r("w_rt_sb", [P, KD, NL])
    b_rt_b = r("b_rt_b", [P, NL])
    stat = r("stat", [P, 3, 32])
    eps = r("eps", [P, 1])
    gidx = r("gidx", [P, SLOTS], I32)
    sidx = r("sidx", [P, SLOTS], I32)
    wgt = r("wgt", [P, SLOTS])
    gidx_cur = r("gidx_cur", [P, 1], I32)
    sidx_cur = r("sidx_cur", [P, 1], I32)
    slot_tab = r("slot_tab", [1, 3 * SLOTS + 1], I32)

    ps = nc.alloc_psum_tensor("ps", [P, 8, 512], F32)

    def sem(name):
        return nc.alloc_semaphore(name)

    param_in = [sem(f"param_in{i}") for i in range(5)]
    g2_in = sem("g2_in")
    g3_in = sem("g3_in")
    x_full = [sem(f"x_full{i}") for i in range(2)]
    wi_full = [sem(f"wi_full{i}") for i in range(ROLES)]
    wo_full = [sem(f"wo_full{i}") for i in range(KD)]
    xr_full = [sem(f"xr_full{i}") for i in range(2)]
    hn_out = [sem(f"hn_out{i}") for i in range(2)]
    st_full = [sem(f"st_full{i}") for i in range(GUC + DNC)]
    consts = sem("consts")
    rconsts = sem("rconsts")
    pool_own = sem("pool_own")
    act_own = sem("act_own")
    dve_own = sem("dve_own")
    eps_ok = sem("eps_ok")
    meta_zero = sem("meta_zero")
    root = sem("root")
    scaled = sem("scaled")
    turned = sem("turned")
    xh_done = sem("xh_done")
    xl_done = sem("xl_done")
    wi_h = sem("wi_h")
    wi_l = sem("wi_l")
    proj = sem("proj")
    ev_act = sem("ev_act")
    ev_dve = sem("ev_dve")
    conv_done = sem("conv_done")
    mean_done = sem("mean_done")
    cent_done = sem("cent_done")
    sq_done = sem("sq_done")
    var_done = sem("var_done")
    std_done = sem("std_done")
    nrm_done = sem("nrm_done")
    silu_done = sem("silu_done")
    wo_h = sem("wo_h")
    wo_l = sem("wo_l")
    mh_done = sem("mh_done")
    ml_done = sem("ml_done")
    op_done = sem("op_done")
    h_done = sem("h_done")
    hroot = sem("hroot")
    hn_done = sem("hn_done")
    hturned = sem("hturned")
    hnt_done = sem("hnt_done")
    rt_done = sem("rt_done")
    lg_done = sem("lg_done")
    exp_in = sem("exp_in")
    exp_out = sem("exp_out")
    a_ready = sem("a_ready")
    ranks = sem("ranks")
    inv_in = sem("inv_in")
    inv_out = sem("inv_out")
    tab_in = sem("tab_in")
    tab_out = sem("tab_out")
    tables = sem("tables")
    gu_h = sem("gu_h")
    gu_l = sem("gu_l")
    dn_h = sem("dn_h")
    dn_l = sem("dn_l")
    gu_used = sem("gu_used")
    dn_used = sem("dn_used")
    idx_ok = sem("idx_ok")
    xg_zero = sem("xg_zero")
    gathered = sem("gathered")
    xt_done = sem("xt_done")
    xt_h = sem("xt_h")
    xt_l = sem("xt_l")
    sil_done = sem("sil_done")
    hid_done = sem("hid_done")
    ht_done = sem("ht_done")
    ht_h = sem("ht_h")
    ht_l = sem("ht_l")
    y_ev = sem("y_ev")
    y_out = sem("y_out")
    ys_full = [sem(f"ys_full{i}") for i in range(NT)]
    z_done = sem("z_done")
    froot = sem("froot")
    o_done = sem("o_done")
    o_out = [sem(f"o_out{i}") for i in range(2)]

    WO_SLOT = [5, 6, 7, 8, 9, 10, 11, 0]
    A0C, BC, FC = 0, 9, 17

    def rows(t):
        return mix[:, :, bass.ds(t * P, P)] if not isinstance(t, int) else mix[:, :, t * P:(t + 1) * P]

    def split8(ap):
        return ap.rearrange("p (k c) -> p k c", c=P)

    block_cm = nc.Block()
    block = block_cm.__enter__()

    @block.sync
    def _(sp):
        sp.wait_ge(meta_zero, 1)
        sp.dma_start(x_in[0:META, 0, :], meta).then_inc(x_full[0], 16)
        sp.dma_start(x_in[:, 1, :], x[0:P, :]).then_inc(x_full[1], 16)
        sp.dma_start(g_mix_b[:], g_mix.partition_broadcast(P)).then_inc(param_in[0], 16)
        for q in (GL, UU):
            sp.dma_start(stage[:, q, :], w_in[q]).then_inc(wi_full[q], 16)
        sp.dma_start(chan_sb[:], chan).then_inc(param_in[1], 16)
        with sp.Fori(0, 3) as i:
            for half in range(2):
                sp.wait_ge(scaled, 2 * i + half + 1)
                sp.dma_start(x_in[:, half, :], x[bass.ds((2 * i + half + 1) * P, P), :]).then_inc(x_full[half], 16)
        sp.wait_ge(scaled, 7)
        sp.dma_start(x_in[:, 0, :], x[7 * P:8 * P, :]).then_inc(x_full[0], 16)
        for q in (CC, VV, BB):
            sp.dma_start(stage[:, q, :], w_in[q]).then_inc(wi_full[q], 16)
        for k in range(KD - 1):
            sp.dma_start(stage[:, WO_SLOT[k], :], w_out[k * P:(k + 1) * P, :]).then_inc(wo_full[k], 16)
        sp.dma_start(w_rt_sb[:], w_rt.rearrange("(k p) n -> p k n", p=P)).then_inc(param_in[2], 16)
        sp.dma_start(b_rt_b[:], b_rt.partition_broadcast(P)).then_inc(param_in[3], 16)
        with sp.Fori(0, NJ - 1) as j:
            for q in range(ROLES):
                sp.wait_ge(wi_l, ROLES * j + q + 1)
                sp.dma_start(stage[:, q, :], w_in[bass.ds(ROLES * j + ROLES + q, 1)].rearrange("a p n -> (a p) n")).then_inc(wi_full[q], 16)
        sp.wait_ge(wi_l, ROLES * NJ)
        sp.dma_start(stage[:, WO_SLOT[7], :], w_out[7 * P:8 * P, :]).then_inc(wo_full[7], 16)
        sp.wait_ge(proj, NJ * ROLES * 3)
        sp.dma_start(g_ffn_b[:], g_ffn.partition_broadcast(P)).then_inc(g2_in, 16)
        for t in range(2):
            sp.dma_start(x_res[:, t, :], x[t * P:(t + 1) * P, :]).then_inc(xr_full[t], 16)

        def load_expert(e, first, n, waits):
            for c in range(first, first + n):
                if waits is not None:
                    s, v = waits
                    sp.wait_ge(s, v + (c - first) + 1)
                if c < GUC:
                    src, q = (w_up if c % 2 else w_gate), c // 2
                    ap = src[e].rearrange("(p k) f -> p (k f)", k=KD)[:, q * D:(q + 1) * D] if isinstance(e, int) else \
                        src[bass.ds(e, 1)].rearrange("a (p k) f -> (a p) (k f)", k=KD)[:, q * D:(q + 1) * D]
                else:
                    q = c - GUC
                    ap = w_down[e].rearrange("(p k) d -> p (k d)", k=KF)[:, q * D:(q + 1) * D] if isinstance(e, int) else \
                        w_down[bass.ds(e, 1)].rearrange("a (p k) d -> (a p) (k d)", k=KF)[:, q * D:(q + 1) * D]
                sp.dma_start(stage[:, c, :], ap).then_inc(st_full[c], 16)

        sp.wait_ge(wo_l, KD)
        load_expert(0, 0, GUC + DNC, None)
        with sp.Fori(0, 3) as i:
            for par in range(2):
                sp.wait_ge(hn_done, 2 * i + par + 1)
                sp.dma_start(hn_rows[bass.ds((2 * i + par) * P, P), :], hn[:, par, :]).then_inc(hn_out[par], 16)
                sp.dma_start(x_res[:, par, :], x[bass.ds((2 * i + par + 2) * P, P), :]).then_inc(xr_full[par], 16)
        for t in (6, 7):
            sp.wait_ge(hn_done, t + 1)
            sp.dma_start(hn_rows[t * P:(t + 1) * P, :], hn[:, t % 2, :]).then_inc(hn_out[t % 2], 16)
        load_expert(1, 0, GUC, (gu_l, 0))
        with sp.Fori(0, NE - 2) as e:
            load_expert(e + 2, 0, GUC, (gu_l, e * GUC + GUC))
            load_expert(e + 1, GUC, DNC, (dn_l, e * DNC))
        load_expert(NE - 1, GUC, DNC, (dn_l, DNC * (NE - 2)))
        sp.wait_ge(tables, 1)
        last = sp.value_load(slot_tab[0:1, 3 * SLOTS:3 * SLOTS + 1], min_val=NE - 1, max_val=SLOTS - 2)
        sp.wait_ge(y_out, last * 16 + 16)
        for t in range(NT):
            for k in range(2):
                sp.dma_start(ys[:, t, k, :], y_rows[k * SEQ + t * P:k * SEQ + (t + 1) * P, :]).then_inc(ys_full[t], 16)
            if t == 0:
                sp.dma_start(g_fin_b[:], g_fin.partition_broadcast(P)).then_inc(g3_in, 16)
        for t in range(NT):
            sp.wait_ge(o_done, t + 1)
            sp.dma_start(out[t * P:(t + 1) * P, :], o_sb[:, t % 2, :]).then_inc(o_out[t % 2], 16)
        for h in range(2):
            sp.wait_ge(o_out[h], 16 * NT // 2)

    @block.gpsimd
    def _(pool):
        own = Tally(pool, pool_own)
        nc.gpsimd.memset(x_in[:, 0, :], 0.0).then_inc(meta_zero, 1)
        own.step(nc.gpsimd.memset(ident[:], 0.0))
        nc.gpsimd.affine_select(out=ident[:], in_=ident[:], compare_op=ALU.not_equal, fill=1.0, base=0,
                                pattern=[[-1, P]], channel_multiplier=1).then_inc(consts, 1)
        nc.gpsimd.memset(ones_cw[:], 1.0 / CW).then_inc(consts, 1)
        for k in range(KD):
            pool.wait_ge(wo_h, k + 1)
            nc.gpsimd.tensor_tensor(wo_lo[:, k, :], stage[:, WO_SLOT[k], :], wo_hi[:, k, :].bitcast(F32),
                                    ALU.subtract).then_inc(wo_l, 1)
        pool.wait_ge(silu_done, 2)
        nc.gpsimd.memset(ones[:], 1.0).then_inc(rconsts, 1)
        own.step(nc.gpsimd.memset(tri[:], 1.0))
        nc.gpsimd.affine_select(out=tri[:], in_=tri[:], compare_op=ALU.is_gt, fill=0.0, base=0,
                                pattern=[[1, P]], channel_multiplier=-1).then_inc(rconsts, 1)
        for ap, pattern, base, cm in (
                (iota_r[:], [[1, P]], 0, 0), (iota_s[:], [[1, SLOTS]], 0, 0), (part[:], [[0, 1]], 0, 1),
                (part1[:], [[0, 1]], 1, 1), (rev[:], [[-1, NEG]], NEG, 0), (thr[:], [[P, 7], [0, NE]], P, 0),
                (asg_id[:], [[SEQ, 2], [P, NT]], 1, 1)):
            nc.gpsimd.iota(ap, pattern=pattern, base=base, channel_multiplier=cm,
                           allow_small_or_imprecise_dtypes=True).then_inc(rconsts, 1)

        pool.wait_ge(tables, 1)
        for h in range(2):
            pool.wait_ge(hn_out[h], 16 * NT // 2)
        nc.gpsimd.memset(x_g[:], 0.0).then_inc(xg_zero, 1)
        last = pool.value_load(slot_tab[0:1, 3 * SLOTS:3 * SLOTS + 1], min_val=NE - 1, max_val=SLOTS - 2)

        pool.wait_ge(xg_zero, 1)
        def column(table, g):
            return table[:, g:g + 1] if isinstance(g, int) else table[:, bass.ds(g, 1)]

        def gather(g, copies):
            if not isinstance(g, int) or g:
                pool.wait_ge(xt_done, g)
            nc.gpsimd.tensor_copy(gidx_cur[:], column(gidx, g)).then_inc(idx_ok, 1)
            pool.wait_ge(idx_ok, copies)
            nc.gpsimd.indirect_dma_start(out=x_g[:], out_offset=None, in_=hn_rows,
                                         in_offset=bass.IndirectOffsetOnAxis(ap=gidx_cur[:, 0:1].bitcast(U32), axis=0),
                                         bounds_check=g + SEQ - 1, oob_is_err=False).then_inc(gathered, 16)

        def scatter(g, copies):
            pool.wait_ge(y_out, g * 16)
            nc.gpsimd.tensor_copy(sidx_cur[:], column(sidx, g)).then_inc(idx_ok, 1)
            pool.wait_ge(idx_ok, copies)
            pool.wait_ge(y_ev, g + 1)
            nc.gpsimd.indirect_dma_start(out=y_rows,
                                         out_offset=bass.IndirectOffsetOnAxis(ap=sidx_cur[:, 0:1].bitcast(U32), axis=0),
                                         in_=y_sb[:], in_offset=None,
                                         bounds_check=g + 2 * SEQ - 1, oob_is_err=False).then_inc(y_out, 16)

        gather(0, 1)
        gather(1, 2)
        with pool.Fori(0, SLOTS - 2) as i:
            with pool.If(i < last):
                gather(i + 2, 2 * i + 3)
                scatter(i, 2 * i + 4)
        scatter(last, 2 * last + 3)

    @block.scalar
    def _(act):
        own = Tally(act, act_own)
        act.wait_ge(eps_ok, 1)

        def mean_root(src, junk_out, column, done):
            ssq = stat[:, 0, bass.ds(column, 1)] if not isinstance(column, int) else stat[:, 0, column:column + 1]
            rt = stat[:, 1, bass.ds(column, 1)] if not isinstance(column, int) else stat[:, 1, column:column + 1]
            own.step(nc.scalar.activation(junk_out, src, ACT.Square, accum_out=ssq))
            nc.scalar.activation(rt, ssq, ACT.Sqrt, bias=eps[:], scale=1.0 / D).then_inc(done, 1)

        def a0_root(n, half):
            if not isinstance(n, int) or n >= 2:
                act.wait_ge(turned, n - 1)
            act.wait_ge(x_full[half], 16 * ((n + (2 - half)) // 2) if isinstance(n, int) else n)
            mean_root(x_in[:, half, :], x_sc[:, half, :], n, root)

        def a0_hi(n, half, t0, w):
            act.wait_ge(turned, n + 1)
            for b in range(2):
                src = ps[:, 2 * half + b, :].rearrange("p (k c) -> p k c", c=P)[:, :, 0:w]
                o = xn_hi[:, 4 * b:4 * b + 4, t0:t0 + w] if isinstance(t0, int) else xn_hi[:, 4 * b:4 * b + 4, bass.ds(t0, w)]
                ins = nc.scalar.copy(o, src)
            ins.then_inc(xh_done, 1)

        def wi_split(q, full):
            act.wait_ge(wi_full[q], full)
            nc.scalar.copy(wi_hi[:, q, :], stage[:, q, :]).then_inc(wi_h, 1)

        a0_root(0, 0)
        wi_split(GL, 16)
        wi_split(UU, 16)
        act.wait_ge(x_full[1], 16)
        mean_root(x_in[:, 1, :], x_sc[:, 1, :], 1, root)
        a0_hi(0, 0, 0, META)
        with act.Fori(0, 3) as i:
            own.loop(i, 2)
            for h in range(2):
                act.wait_ge(turned, 2 * i + h + 1)
                act.wait_ge(x_full[h], 16 * i + 32)
                mean_root(x_in[:, h, :], x_sc[:, h, :], 2 * i + 2 + h, root)
                a0_hi(2 * i + 1 + h, 1 - h, (2 * i + h) * P + META, P)
            own.end(3)
        act.wait_ge(turned, 7)
        act.wait_ge(x_full[0], 16 * 5)
        mean_root(x_in[:, 0, :], x_sc[:, 0, :], 8, root)
        a0_hi(7, 1, 6 * P + META, P)
        a0_hi(8, 0, 7 * P + META, P)
        for q in (CC, VV, BB):
            wi_split(q, 16)

        def body_a(j, split_next):
            for b, (t0, n) in enumerate(BLK):
                act.wait_ge(proj, 15 * j + b + 1)
                nc.scalar.activation(sig[:, t0:t0 + n], ps[:, b, 0:n], ACT.Sigmoid).then_inc(ev_act, 1)
            if split_next:
                wi_split(GL, 16 * j + 32)
                act.wait_ge(proj, 15 * j + 6)
                wi_split(UU, 16 * j + 32)
            for b, (t0, n) in enumerate(BLK):
                act.wait_ge(proj, 15 * j + 6 + b + 1)
                nc.scalar.copy(c_sb[:, t0:t0 + n], ps[:, b, 0:n]).then_inc(ev_act, 1)
            if split_next:
                wi_split(CC, 16 * j + 32)
                act.wait_ge(proj, 15 * j + 12)
                wi_split(VV, 16 * j + 32)
                act.wait_ge(proj, 15 * j + 15)
                wi_split(BB, 16 * j + 32)

        with act.Fori(0, NJ - 1) as j:
            body_a(j, True)
        body_a(NJ - 1, False)
        act.wait_ge(proj, NJ * 15)
        for k in range(KD):
            act.wait_ge(wo_full[k], 16)
            nc.scalar.copy(wo_hi[:, k, :], stage[:, WO_SLOT[k], :]).then_inc(wo_h, 1)

        for h in range(2):
            cols = slice(512 * h, 512 * h + 512)
            act.wait_ge(cent_done, h + 1)
            if h:
                act.wait_ge(var_done, h)
            for j in range(NJ):
                ins = nc.scalar.activation(sq[:, j, :], mix[:, j, cols], ACT.Square)
            ins.then_inc(sq_done, 1)
            act.wait_ge(var_done, h + 1)
            if h:
                act.wait_ge(nrm_done, h)
            nc.scalar.activation(std[:], ps[:, 2 + h, :], ACT.Sqrt, bias=eps[:]).then_inc(std_done, 1)
        for h in range(2):
            cols = slice(512 * h, 512 * h + 512)
            act.wait_ge(nrm_done, h + 1)
            for j in range(NJ):
                c = j * NCH
                ins = nc.scalar.activation(mix[:, j, cols], mix[:, j, cols], ACT.Silu, bias=chan_sb[:, c + LB:c + LB + 1],
                                           scale=chan_sb[:, c + LG:c + LG + 1])
            ins.then_inc(silu_done, 1)

        def m_split(t, par):
            if not isinstance(t, int) or t >= 2:
                act.wait_ge(op_done, t - 1)
            nc.scalar.copy(m_hi[:, par], rows(t)).then_inc(mh_done, 1)

        def b_root(t, par):
            act.wait_ge(h_done, t + 1)
            if isinstance(t, int):
                if t >= 2:
                    act.wait_ge(hn_out[par], 16 * (t // 2))
            else:
                act.wait_ge(hn_out[par], (t - par) * 8)
            mean_root(rows(t), split8(hn[:, par, :]), t + BC, hroot)

        def hnt_copy(t):
            act.wait_ge(hturned, t + 1)
            if not isinstance(t, int) or t >= 1:
                act.wait_ge(rt_done, t)
            for b in range(2):
                ins = nc.scalar.copy(hn_t[:, 4 * b:4 * b + 4, :], ps[:, 4 + b, :].rearrange("p (k c) -> p k c", c=P))
            ins.then_inc(hnt_done, 1)

        act.wait_ge(silu_done, 2)
        act.wait_ge(ev_dve, 3 + 9 * NJ)
        m_split(0, 0)
        m_split(1, 1)
        b_root(0, 0)
        with act.Fori(0, 3) as i:
            own.loop(i, 2)
            for k in range(2):
                m_split(2 * i + 2 + k, k)
                act.wait_ge(hturned, 2 * i + k + 1)
                act.wait_ge(rt_done, 2 * i + k)
                for b in range(2):
                    ins = nc.scalar.copy(hn_t[:, 4 * b:4 * b + 4, :], ps[:, 4 + b, :].rearrange("p (k c) -> p k c", c=P))
                ins.then_inc(hnt_done, 1)
                par = 1 - k
                act.wait_ge(h_done, 2 * i + k + 2)
                act.wait_ge(hn_out[par], 16 * i + 16 * k)
                mean_root(rows(2 * i + 1 + k), split8(hn[:, par, :]), 2 * i + 1 + k + BC, hroot)
            own.end(3)
        hnt_copy(6)
        b_root(7, 1)
        hnt_copy(7)

        act.wait_ge(exp_in, 1)
        nc.scalar.activation(g_ex[:], g_sh[:], ACT.Exp).then_inc(exp_out, 1)
        act.wait_ge(exp_in, 2)
        nc.scalar.activation(vec[:, 5, :], vec[:, 4, :], ACT.Exp).then_inc(exp_out, 1)

        def gu_split(e1, c, used):
            if used is not None:
                act.wait_ge(gu_used, used + c + 1)
            act.wait_ge(st_full[c], e1 * 16 + 16)
            nc.scalar.copy(gu_hi[:, c, :], stage[:, c, :]).then_inc(gu_h, 1)

        def xt_copy(count):
            act.wait_ge(xt_done, count)
            for b in range(2):
                ins = nc.scalar.copy(xt_hi[:, 4 * b:4 * b + 4, :], ps[:, 4 + b, :].rearrange("p (k c) -> p k c", c=P))
            ins.then_inc(xt_h, 1)

        def ht_copy(s):
            act.wait_ge(ht_done, s + 1)
            act.wait_ge(dn_used, s * DNC)
            nc.scalar.copy(ht_hi[:], ps[:, 6, :].rearrange("p (k c) -> p k c", c=P)).then_inc(ht_h, 1)

        def y_copy(s):
            act.wait_ge(dn_used, s * DNC + DNC)
            act.wait_ge(y_out, s * 16)
            for n in range(2):
                ins = nc.scalar.activation(y_sb[:, 512 * n:512 * n + 512], ps[:, 2 + n, :], ACT.Copy,
                                           scale=wgt[:, bass.ds(s, 1)])
            ins.then_inc(y_ev, 1)

        act.wait_ge(op_done, NT)
        for c in range(GUC):
            gu_split(0, c, None)
        act.wait_ge(tables, 1)
        last = act.value_load(slot_tab[0:1, 3 * SLOTS:3 * SLOTS + 1], min_val=NE - 1, max_val=SLOTS - 2)

        def body_c(s, first_step):
            g = 0 if first_step else s + 1
            e = act.value_load(slot_tab[0:1, bass.ds(g, 1)], min_val=0, max_val=NE - 1) if not first_step else 0
            beg = act.value_load(slot_tab[0:1, bass.ds(g + SLOTS, 1)], min_val=0, max_val=1) if not first_step else 1
            end = act.value_load(slot_tab[0:1, bass.ds(g + 2 * SLOTS, 1)] if not first_step else
                                 slot_tab[0:1, 2 * SLOTS:2 * SLOTS + 1], min_val=0, max_val=1)
            with act.If(end > 0):
                for c in range(GUC):
                    gu_split(e + 1, c, g * GUC)
                    if c == 3 and not first_step:
                        ht_copy(s)
            with act.Else():
                if not first_step:
                    ht_copy(s)
                else:
                    act.wait_ge(gu_used, 1)
            act.wait_ge(gu_used, g * GUC + GUC)
            nc.scalar.activation(sil[:], ps[:, 0, :], ACT.Silu).then_inc(sil_done, 1)
            xt_copy(g + 2)
            def dn_split():
                for c in range(DNC):
                    if not first_step:
                        act.wait_ge(dn_used, s * DNC + c + 1)
                    act.wait_ge(st_full[GUC + c], e * 16 + 16)
                    nc.scalar.copy(dn_hi[:, c, :], stage[:, GUC + c, :]).then_inc(dn_h, 1)
            if first_step:
                dn_split()
            else:
                with act.If(beg > 0):
                    dn_split()
                y_copy(s)

        xt_copy(1)
        body_c(None, True)
        with act.Fori(0, SLOTS - 2) as s:
            with act.If(s < last):
                body_c(s, False)
        ht_copy(last)
        y_copy(last)

        for t in range(NT):
            act.wait_ge(z_done, t + 1)
            own.step(nc.scalar.activation(f_sq[:], z[:, t % 2, :], ACT.Square, accum_out=stat[:, 0, FC + t:FC + t + 1]))
            nc.scalar.activation(stat[:, 1, FC + t:FC + t + 1], stat[:, 0, FC + t:FC + t + 1], ACT.Sqrt, bias=eps[:],
                                 scale=1.0 / D).then_inc(froot, 1)

    @block.vector
    def _(dve):
        own = Tally(dve, dve_own)
        v = nc.vector
        v.memset(eps[:], EPS).then_inc(eps_ok, 1)
        v.memset(a_buf[:, 0:PAD], 0.0).then_inc(ev_dve, 3)

        def a0_scale(n, half):
            col = (lambda k: stat[:, k, bass.ds(n, 1)]) if not isinstance(n, int) else (lambda k: stat[:, k, n:n + 1])
            dve.wait_ge(root, n + 1)
            own.step(v.reciprocal(col(2), col(1)))
            v.scalar_tensor_tensor(out=x_sc[:, half, :], in0=x_in[:, half, :], scalar=col(2), in1=g_mix_b[:],
                                   op0=ALU.mult, op1=ALU.mult).then_inc(scaled, 1)

        def a0_lo(n, half, t0, w):
            dve.wait_ge(xh_done, n + 1)
            for b in range(2):
                src = ps[:, 2 * half + b, :].rearrange("p (k c) -> p k c", c=P)[:, :, 0:w]
                if isinstance(t0, int):
                    hi, lo = (a[:, 4 * b:4 * b + 4, t0:t0 + w] for a in (xn_hi, xn_lo))
                else:
                    hi, lo = (a[:, 4 * b:4 * b + 4, bass.ds(t0, w)] for a in (xn_hi, xn_lo))
                ins = v.tensor_tensor(lo, src, hi.bitcast(F32), ALU.subtract)
            ins.then_inc(xl_done, 1)

        def wi_low(q, count):
            dve.wait_ge(wi_h, count)
            v.tensor_tensor(wi_lo[:, q, :], stage[:, q, :], wi_hi[:, q, :].bitcast(F32), ALU.subtract).then_inc(wi_l, 1)

        dve.wait_ge(param_in[0], 16)
        a0_scale(0, 0)
        wi_low(GL, 1)
        wi_low(UU, 2)
        a0_scale(1, 1)
        a0_lo(0, 0, 0, META)
        with dve.Fori(0, 3) as i:
            own.loop(i, 2)
            for h in range(2):
                a0_scale(2 * i + 2 + h, h)
                a0_lo(2 * i + 1 + h, 1 - h, (2 * i + h) * P + META, P)
            own.end(3)
        a0_scale(8, 0)
        a0_lo(7, 1, 6 * P + META, P)
        a0_lo(8, 0, 7 * P + META, P)
        for q in (CC, VV, BB):
            wi_low(q, q + 1)
        dve.wait_ge(param_in[1], 16)

        def body_a(j, split_next):
            def const(k):
                return chan_sb[:, bass.ds(j * NCH + k, 1)] if not isinstance(j, int) else chan_sb[:, j * NCH + k:j * NCH + k + 1]

            def line(off):
                if isinstance(j, int):
                    return mix[:, off + j, :]
                return mix[:, bass.ds(j + off, 1), :].rearrange("p a t -> p (a t)")

            def taps(lo, hi):
                y = line(0)
                for k in range(lo, hi):
                    src = a_buf[:, k:k + SEQ]
                    if k == 0:
                        ins = v.tensor_scalar(y, src, const(0), const(CB), ALU.mult, ALU.add)
                    else:
                        ins = v.scalar_tensor_tensor(out=y, in0=src, scalar=const(k), in1=y, op0=ALU.mult, op1=ALU.add)
                    if k == TAPS - 1:
                        ins.then_inc(conv_done, 1)
                        dve.wait_ge(conv_done, j + 1)
                    else:
                        own.step(ins)

            def low(q):
                if split_next:
                    wi_low(q, ROLES * j + ROLES + q + 1)

            low(GL)
            for b, (t0, n) in enumerate(BLK):
                dve.wait_ge(ev_act, 6 * j + b + 1)
                dve.wait_ge(proj, 15 * j + 3 + b + 1)
                v.tensor_tensor(a_buf[:, PAD + t0:PAD + t0 + n], ps[:, 3 + b, 0:n], sig[:, t0:t0 + n],
                                ALU.mult).then_inc(ev_dve, 1)
            low(UU)
            dve.wait_ge(ev_dve, 9 * j + 6)
            taps(0, 6)
            low(CC)
            taps(6, 11)
            for b, (t0, n) in enumerate(BLK):
                dve.wait_ge(ev_act, 6 * j + 3 + b + 1)
                dve.wait_ge(proj, 15 * j + 9 + b + 1)
                v.tensor_tensor(cv[:, t0:t0 + n], ps[:, 3 + b, 0:n], c_sb[:, t0:t0 + n], ALU.mult).then_inc(ev_dve, 1)
            low(VV)
            dve.wait_ge(ev_dve, 9 * j + 9)
            s = line(NJ)
            for k in range(STAPS):
                src = cv[:, META - STAPS + 1 + k:META - STAPS + 1 + k + SEQ]
                if k == 0:
                    own.step(v.tensor_scalar(s, src, const(SW), None, ALU.mult))
                else:
                    own.step(v.scalar_tensor_tensor(out=s, in0=src, scalar=const(SW + k), in1=s, op0=ALU.mult, op1=ALU.add))
            taps(11, 13)
            for b, (t0, n) in enumerate(BLK):
                dve.wait_ge(proj, 15 * j + 12 + b + 1)
                skip = META if b == 0 else 0
                o = t0 + skip - META
                if isinstance(j, int):
                    seg = mix[:, NJ + j, o:o + n - skip]
                else:
                    seg = mix[:, bass.ds(j + NJ, 1), o:o + n - skip].rearrange("p a t -> p (a t)")
                v.tensor_tensor(seg, ps[:, b, skip:n], seg, ALU.mult).then_inc(ev_dve, 1)
            low(BB)
            taps(13, TAPS)

        with dve.Fori(0, NJ - 1) as j:
            own.loop(j, TAPS - 1 + STAPS)
            body_a(j, True)
            own.end(NJ - 1)
        body_a(NJ - 1, False)

        for h in range(2):
            cols = slice(512 * h, 512 * h + 512)
            dve.wait_ge(mean_done, h + 1)
            for j in range(NJ):
                ins = v.tensor_tensor(mix[:, j, cols], mix[:, j, cols], ps[:, h, :], ALU.subtract)
            ins.then_inc(cent_done, 1)
        for h in range(2):
            cols = slice(512 * h, 512 * h + 512)
            dve.wait_ge(std_done, h + 1)
            own.step(v.reciprocal(rstd[:], std[:]))
            dve.wait_ge(sq_done, h + 1)
            for j in range(NJ):
                ins = v.tensor_tensor(mix[:, j, cols], mix[:, j, cols], rstd[:], ALU.mult)
            ins.then_inc(nrm_done, 1)
            dve.wait_ge(nrm_done, h + 1)

        def m_low(t, par):
            dve.wait_ge(mh_done, t + 1)
            v.tensor_tensor(m_lo[:, par], rows(t), m_hi[:, par].bitcast(F32), ALU.subtract).then_inc(ml_done, 1)

        def h_rows(t, par, full):
            dve.wait_ge(xr_full[par], full)
            dve.wait_ge(op_done, t + 1)
            hs = rows(t)
            for b in range(2):
                ins = v.tensor_tensor(hs[:, 4 * b:4 * b + 4, :], split8(ps[:, 2 * par + b, :]),
                                      split8(x_res[:, par, 512 * b:512 * b + 512]), ALU.add)
            ins.then_inc(h_done, 1)

        def hn_rows_of(t, par):
            col = (lambda k: stat[:, k, bass.ds(t + BC, 1)]) if not isinstance(t, int) else (lambda k: stat[:, k, BC + t:BC + t + 1])
            dve.wait_ge(hroot, t + 1)
            own.step(v.reciprocal(col(2), col(1)))
            v.scalar_tensor_tensor(out=hn[:, par, :], in0=rows(t), scalar=col(2), in1=g_ffn_b[:],
                                   op0=ALU.mult, op1=ALU.mult).then_inc(hn_done, 1)

        def logits(t):
            dve.wait_ge(rt_done, t + 1)
            o = logit[:, bass.ds(t, 1), :].rearrange("p a n -> p (a n)") if not isinstance(t, int) else logit[:, t, :]
            v.tensor_tensor(o, ps[:, 6, 0:NL], b_rt_b[:], ALU.add).then_inc(lg_done, 1)

        dve.wait_ge(g2_in, 16)
        dve.wait_ge(param_in[3], 16)
        m_low(0, 0)
        m_low(1, 1)
        h_rows(0, 0, 16)
        hn_rows_of(0, 0)
        with dve.Fori(0, 3) as i:
            own.loop(i, 2)
            for k in range(2):
                m_low(2 * i + 2 + k, k)
                h_rows(2 * i + 1 + k, 1 - k, 16 * i + 16 + 16 * k)
                hn_rows_of(2 * i + 1 + k, 1 - k)
                logits(2 * i + k)
            own.end(3)
        h_rows(7, 1, 64)
        hn_rows_of(7, 1)
        logits(6)
        logits(7)
        dve.wait_ge(lg_done, NT)

        dve.wait_ge(rconsts, 9)
        step = own.step
        lg_g = logit[:, :, 0:NG]
        lg_e = logit[:, :, NG:NL].rearrange("p t (g e) -> p t g e", g=NG)

        def spread(ap, n):
            return ap.unsqueeze(2).broadcast_to([P, ap.shape[1], n])

        def over_tiles(ap, n=NT):
            return ap.unsqueeze(1).broadcast_to([P, n, ap.shape[1]])

        m_g, m_1, m_2, k_m, diff, q_e, g_sum, g_top, den, r_den = (vec[:, k, :] for k in range(10))
        step(v.tensor_reduce(m_g, lg_g, AX.X, ALU.max))
        v.tensor_tensor(g_sh[:], lg_g, spread(m_g, NG), ALU.subtract).then_inc(exp_in, 1)

        def first_max(src, top, n, keybuf, onehot):
            step(v.tensor_tensor(keybuf, src, spread(top, n), ALU.is_equal))
            step(v.tensor_tensor(keybuf, keybuf, over_tiles(rev[:, NEG - n:NEG]), ALU.mult))
            step(v.tensor_reduce(k_m, keybuf, AX.X, ALU.max))
            step(v.tensor_tensor(onehot, keybuf, spread(k_m, n), ALU.is_equal))

        first_max(lg_g, m_g, NG, g_key[:], g_one[:])
        one4 = g_one[:].unsqueeze(3).broadcast_to([P, NT, NG, NEG])
        step(v.tensor_tensor(a1[:], lg_e, one4, ALU.mult))
        step(v.tensor_reduce(sel[:], a1[:].rearrange("p t g e -> p t e g"), AX.X, ALU.add))
        step(v.tensor_reduce(m_1, sel[:], AX.X, ALU.max))
        first_max(sel[:], m_1, NEG, key[:], o1[:])
        step(v.scalar_tensor_tensor(out=sel2[:], in0=o1[:], scalar=-3.0e38, in1=sel[:], op0=ALU.mult, op1=ALU.add))
        step(v.tensor_reduce(m_2, sel2[:], AX.X, ALU.max))
        v.tensor_tensor(diff, m_2, m_1, ALU.subtract).then_inc(exp_in, 1)
        first_max(sel2[:], m_2, NEG, key[:], o2[:])
        for a, o in ((a1, o1), (a2, o2)):
            step(v.tensor_tensor(a[:], o[:].unsqueeze(2).broadcast_to([P, NT, NG, NEG]), one4, ALU.mult))
        flat1, flat2 = (a[:].rearrange("p t g e -> p t (g e)") for a in (a1, a2))
        v.tensor_tensor(a12[:], flat1, flat2, ALU.add).then_inc(a_ready, 1)
        dve.wait_ge(exp_out, 2)
        step(v.tensor_reduce(g_sum, g_ex[:], AX.X, ALU.add))
        step(v.reciprocal(g_top, g_sum))
        step(v.tensor_scalar(den, q_e, 1.0, None, ALU.add))
        step(v.reciprocal(r_den, den))
        step(v.tensor_tensor(wk[:, 0, :], g_top, r_den, ALU.mult))
        step(v.tensor_tensor(wk[:, 1, :], wk[:, 0, :], q_e, ALU.mult))
        step(v.memset(before[:, 0, :], 0.0))
        dve.wait_ge(ranks, 1)
        tot = ps[:, 7, 256:512].rearrange("p (t e) -> p t e", e=NE)
        for t in range(NT):
            step(v.tensor_tensor(before[:, t + 1, :], tot[:, t, :], before[:, t, :], ALU.add))
        step(v.tensor_tensor(pos[:], ps[:, 7, 0:256].rearrange("p (t e) -> p t e", e=NE), before[:, 0:NT, :], ALU.add))
        step(v.tensor_tensor(more[:], over_tiles(before[:, NT, :], 7), thr[:], ALU.is_gt))
        step(v.tensor_reduce(nblk[:], more[:].rearrange("p b e -> p e b"), AX.X, ALU.add))
        step(v.tensor_scalar(nblk[:], nblk[:], 1.0, None, ALU.add))
        step(v.tensor_tensor_scan(s_end[:], ones[:, 0:NE], nblk[:], 0.0, ALU.mult, ALU.add))
        step(v.tensor_tensor(s_beg[:], s_end[:], nblk[:], ALU.subtract))
        step(v.tensor_scalar(junk[:], s_end[:], part[:], 0.0, ALU.is_le, ALU.add, accum_out=tab[:, 0:1]))
        step(v.tensor_scalar(junk[:], s_beg[:], part[:], 0.0, ALU.is_equal, ALU.add, accum_out=tab[:, 1:2]))
        step(v.tensor_scalar(junk[:, 0:NE - 1], s_end[:, 0:NE - 1], part1[:], 0.0, ALU.is_equal, ALU.add, accum_out=tab[:, 2:3]))
        step(v.tensor_scalar(tab[:, 0:1], tab[:, 0:1], float(NE - 1), None, ALU.min))
        v.tensor_scalar(slot_tab[0:1, 3 * SLOTS:3 * SLOTS + 1], s_end[0:1, NE - 1:NE], -1.0, None, ALU.add).then_inc(tab_in, 1)
        step(v.scalar_tensor_tensor(out=dest[:], in0=over_tiles(s_beg[:]), scalar=float(P), in1=pos[:],
                                    op0=ALU.mult, op1=ALU.add))
        for k, a in enumerate((flat1, flat2)):
            step(v.tensor_tensor(prod[:], dest[:], a, ALU.mult))
            step(v.tensor_reduce(dd[:, k, :], prod[:], AX.X, ALU.add))
        step(v.tensor_copy(dd_i[:], dd[:]))
        step(v.tensor_scalar(sl_i[:], dd_i[:], 7, None, ALU.arith_shift_right))
        step(v.tensor_scalar(ro_i[:], dd_i[:], P - 1, None, ALU.bitwise_and))
        step(v.tensor_copy(sl_f[:], sl_i[:]))
        step(v.tensor_copy(ro_f[:], ro_i[:]))
        v.tensor_tensor(one_r[:], over_tiles(iota_r[:], 2 * NT), spread(ro_f[:].rearrange("p k t -> p (k t)"), P), ALU.is_equal).then_inc(inv_in, 1)
        step(v.tensor_tensor(one_s[:], over_tiles(iota_s[:], 2 * NT), spread(sl_f[:].rearrange("p k t -> p (k t)"), SLOTS), ALU.is_equal))
        for k, a in enumerate((asg_id, wk)):
            v.tensor_tensor(val_s[:, :, k, :], one_s[:], spread(a[:].rearrange("p k t -> p (k t)"), SLOTS), ALU.mult).then_inc(inv_in, 1)
        dve.wait_ge(inv_out, 1)
        step(v.tensor_scalar(vm[:], ps[:, 6, 0:SLOTS], -1.0, None, ALU.add))
        step(v.tensor_scalar(inv[:], ps[:, 6, 0:SLOTS], 0.0, float(OOB), ALU.is_equal, ALU.mult))
        step(v.tensor_copy(wgt[:], ps[:, 6, SLOTS:2 * SLOTS]))
        step(v.tensor_scalar(v_f[:], vm[:], 0.0, None, ALU.max))
        step(v.tensor_copy(v_i[:], v_f[:]))
        step(v.tensor_scalar(v_i[:], v_i[:], SEQ - 1, None, ALU.bitwise_and))
        step(v.tensor_copy(v_f[:], v_i[:]))
        step(v.tensor_tensor(gidx[:], v_f[:], inv[:], ALU.add))
        step(v.tensor_tensor(sidx[:], vm[:], inv[:], ALU.add))
        dve.wait_ge(tab_out, 1)
        v.tensor_copy(slot_tab[0:1, 0:3 * SLOTS].rearrange("p (k s) -> p k s", s=SLOTS),
                      ps[0:1, 5, 0:3 * P].rearrange("p (k s) -> p k s", s=P)[:, :, 0:SLOTS]).then_inc(tables, 1)

        def gu_low(e1, c):
            dve.wait_ge(gu_h, e1 * GUC + c + 1)
            v.tensor_tensor(gu_lo[:, c, :], stage[:, c, :], gu_hi[:, c, :].bitcast(F32), ALU.subtract).then_inc(gu_l, 1)

        def xt_low(count):
            dve.wait_ge(xt_h, count)
            for b in range(2):
                ins = v.tensor_tensor(xt_lo[:, 4 * b:4 * b + 4, :], split8(ps[:, 4 + b, :]),
                                      xt_hi[:, 4 * b:4 * b + 4, :].bitcast(F32), ALU.subtract)
            ins.then_inc(xt_l, 1)

        def ht_low(s):
            dve.wait_ge(ht_h, s + 1)
            v.tensor_tensor(ht_lo[:], split8(ps[:, 6, :]), ht_hi[:].bitcast(F32), ALU.subtract).then_inc(ht_l, 1)

        for c in range(GUC):
            gu_low(0, c)
        dve.wait_ge(tables, 1)
        last = dve.value_load(slot_tab[0:1, 3 * SLOTS:3 * SLOTS + 1], min_val=NE - 1, max_val=SLOTS - 2)

        def body_c(s, first_step):
            g = 0 if first_step else s + 1
            e = dve.value_load(slot_tab[0:1, bass.ds(g, 1)], min_val=0, max_val=NE - 1) if not first_step else 0
            beg = dve.value_load(slot_tab[0:1, bass.ds(g + SLOTS, 1)], min_val=0, max_val=1) if not first_step else 1
            end = dve.value_load(slot_tab[0:1, bass.ds(g + 2 * SLOTS, 1)] if not first_step else
                                 slot_tab[0:1, 2 * SLOTS:2 * SLOTS + 1], min_val=0, max_val=1)
            with dve.If(end > 0):
                for c in range(GUC):
                    gu_low(e + 1, c)
                    if c == 3 and not first_step:
                        ht_low(s)
            with dve.Else():
                if not first_step:
                    ht_low(s)
                else:
                    dve.wait_ge(gu_used, 1)
            dve.wait_ge(sil_done, g + 1)
            v.tensor_tensor(hid[:], ps[:, 1, :], sil[:], ALU.mult).then_inc(hid_done, 1)
            xt_low(g + 2)

            def dn_low():
                for c in range(DNC):
                    dve.wait_ge(dn_h, e * DNC + c + 1)
                    v.tensor_tensor(dn_lo[:, c, :], stage[:, GUC + c, :], dn_hi[:, c, :].bitcast(F32),
                                    ALU.subtract).then_inc(dn_l, 1)
            if first_step:
                dn_low()
            else:
                with dve.If(beg > 0):
                    dn_low()
                dve.nop()

        xt_low(1)
        body_c(None, True)
        with dve.Fori(0, SLOTS - 2) as s:
            with dve.If(s < last):
                body_c(s, False)
        ht_low(last)

        def f_out(t):
            par = t % 2
            dve.wait_ge(froot, t + 1)
            step(v.reciprocal(stat[:, 2, FC + t:FC + t + 1], stat[:, 1, FC + t:FC + t + 1]))
            if t >= 2:
                dve.wait_ge(o_out[par], 16 * (t // 2))
            v.scalar_tensor_tensor(out=o_sb[:, par, :], in0=z[:, par, :], scalar=stat[:, 2, FC + t:FC + t + 1],
                                   in1=g_fin_b[:], op0=ALU.mult, op1=ALU.mult).then_inc(o_done, 1)

        dve.wait_ge(g3_in, 16)
        for t in range(NT):
            par = t % 2
            dve.wait_ge(ys_full[t], 32)
            if t >= 2:
                dve.wait_ge(o_done, t - 1)
            step(v.tensor_tensor(split8(z[:, par, :]), rows(t), split8(ys[:, t, 0, :]), ALU.add))
            v.tensor_tensor(z[:, par, :], z[:, par, :], ys[:, t, 1, :], ALU.add).then_inc(z_done, 1)
            if t >= 1:
                f_out(t - 1)
        f_out(NT - 1)

    @block.tensor
    def _(pe):
        mm = nc.tensor.matmul

        def three(o, s_hi, s_lo, m_hi_, m_lo_, start, stop):
            mm(o, s_hi, m_hi_, start=start, stop=False)
            mm(o, s_hi, m_lo_, start=False, stop=False)
            return mm(o, s_lo, m_hi_, start=False, stop=stop)

        pe.wait_ge(consts, 2)

        def turn(src, banks, step_k):
            for k in range(KD):
                ins = nc.tensor.transpose(ps[:, banks + k // 4, (k % 4) * P:(k % 4 + 1) * P],
                                          src[:, k:D:KD] if step_k else src[:, k * P:(k + 1) * P], ident[:])
            return ins

        def a0_turn(n, half):
            pe.wait_ge(scaled, n + 1)
            if not isinstance(n, int) or n >= 2:
                pe.wait_ge(xl_done, n - 1)
            turn(x_sc[:, half, :], 2 * half, False).then_inc(turned, 1)

        a0_turn(0, 0)
        a0_turn(1, 1)
        with pe.Fori(0, 3) as i:
            for h in range(2):
                a0_turn(2 * i + 2 + h, h)
        a0_turn(8, 0)
        pe.wait_ge(xl_done, 9)

        with pe.Fori(0, NJ) as j:
            for q in range(ROLES):
                pe.wait_ge(wi_l, ROLES * j + q + 1)
                for b, (t0, n) in enumerate(BLK):
                    if q == GL:
                        pe.wait_ge(ev_dve, 9 * j + b + 1)
                    elif q == CC:
                        pe.wait_ge(ev_act, 6 * j + b + 1)
                    elif q == VV:
                        pe.wait_ge(ev_dve, 9 * j + 3 + b + 1)
                    elif q == BB:
                        pe.wait_ge(ev_act, 6 * j + 3 + b + 1)
                    for k in range(KD):
                        ins = three(ps[:, 3 * (q % 2) + b, 0:n], wi_hi[:, q, k * P:(k + 1) * P], wi_lo[:, q, k * P:(k + 1) * P],
                                    xn_hi[:, k, t0:t0 + n], xn_lo[:, k, t0:t0 + n], k == 0, k == KD - 1)
                    ins.then_inc(proj, 1)

        pe.wait_ge(conv_done, NJ)
        pe.wait_ge(ev_dve, 3 + 9 * NJ)
        for h in range(2):
            for j in range(NJ):
                ins = mm(ps[:, h, :], ones_cw[:], mix[:, j, 512 * h:512 * h + 512], start=j == 0, stop=j == NJ - 1)
            ins.then_inc(mean_done, 1)
        for h in range(2):
            pe.wait_ge(sq_done, h + 1)
            for j in range(NJ):
                ins = mm(ps[:, 2 + h, :], ones_cw[:], sq[:, j, :], start=j == 0, stop=j == NJ - 1)
            ins.then_inc(var_done, 1)

        def out_proj(t, par):
            pe.wait_ge(ml_done, t + 1)
            if not isinstance(t, int) or t >= 2:
                pe.wait_ge(h_done, t - 1)
            for b in range(2):
                for k in range(KD):
                    ins = three(ps[:, 2 * par + b, :], m_hi[:, par, k, :], m_lo[:, par, k, :],
                                wo_hi[:, k, 512 * b:512 * b + 512], wo_lo[:, k, 512 * b:512 * b + 512], k == 0, k == KD - 1)
            ins.then_inc(op_done, 1)

        def turn_h(t, par):
            pe.wait_ge(hn_done, t + 1)
            if not isinstance(t, int) or t >= 1:
                pe.wait_ge(hnt_done, t)
            turn(hn[:, par, :], 4, False).then_inc(hturned, 1)

        def router(t):
            pe.wait_ge(hnt_done, t + 1)
            if not isinstance(t, int) or t >= 1:
                pe.wait_ge(lg_done, t)
            for k in range(KD):
                ins = mm(ps[:, 6, 0:NL], hn_t[:, k, :], w_rt_sb[:, k, :], start=k == 0, stop=k == KD - 1)
            ins.then_inc(rt_done, 1)

        pe.wait_ge(wo_l, KD)
        pe.wait_ge(param_in[2], 16)
        out_proj(0, 0)
        out_proj(1, 1)
        turn_h(0, 0)
        with pe.Fori(0, 3) as i:
            for k in range(2):
                out_proj(2 * i + 2 + k, k)
                router(2 * i + k)
                turn_h(2 * i + 1 + k, 1 - k)
        router(6)
        turn_h(7, 1)
        router(7)

        pe.wait_ge(rconsts, 9)
        pe.wait_ge(a_ready, 1)
        a_all = a12[:].rearrange("p t e -> p (t e)")
        mm(ps[:, 7, 0:256], tri[:], a_all, start=True, stop=True)
        mm(ps[:, 7, 256:512], ones[:], a_all, start=True, stop=True).then_inc(ranks, 1)
        pe.wait_ge(tab_in, 1)
        for k in range(3):
            ins = mm(ps[0:1, 5, k * P:(k + 1) * P], tab[:, k:k + 1], ident[:], start=True, stop=True)
        ins.then_inc(tab_out, 1)
        pe.wait_ge(inv_in, 3)
        for a in range(2 * NT):
            ins = mm(ps[:, 6, 0:2 * SLOTS], one_r[:, a, :], val_s[:, a].rearrange("p k s -> p (k s)"),
                     start=a == 0, stop=a == 2 * NT - 1)
        ins.then_inc(inv_out, 1)

        def turn_x(count):
            pe.wait_ge(gathered, count * 16)
            turn(x_g[:], 4, True).then_inc(xt_done, 1)

        def turn_hid(s):
            pe.wait_ge(hid_done, s + 1)
            pe.wait_ge(ht_l, s)
            for k in range(KF):
                ins = nc.tensor.transpose(ps[:, 6, k * P:(k + 1) * P], hid[:, k:F:KF], ident[:])
            ins.then_inc(ht_done, 1)

        def gate_up(g, e, middle):
            pe.wait_ge(xt_l, g + 1)
            if middle is not None:
                pe.wait_ge(hid_done, middle + 1)
            for c in range(GUC):
                pe.wait_ge(gu_l, e * GUC + c + 1)
                for kk in range(2):
                    k = 2 * (c // 2) + kk
                    cols = slice(512 * kk, 512 * kk + 512)
                    ins = three(ps[:, c % 2, :], xt_hi[:, k, :], xt_lo[:, k, :], gu_hi[:, c, cols], gu_lo[:, c, cols],
                                k == 0, k == KD - 1)
                ins.then_inc(gu_used, 1)
                if c == 3 and middle is not None:
                    turn_hid(middle)

        def down(s, e):
            pe.wait_ge(ht_l, s + 1)
            pe.wait_ge(y_ev, s)
            for c in range(DNC):
                pe.wait_ge(dn_l, e * DNC + c + 1)
                for n in range(2):
                    cols = slice(512 * n, 512 * n + 512)
                    ins = three(ps[:, 2 + n, :], ht_hi[:, c, :], ht_lo[:, c, :], dn_hi[:, c, cols], dn_lo[:, c, cols],
                                c == 0, c == DNC - 1)
                ins.then_inc(dn_used, 1)

        pe.wait_ge(tables, 1)
        last = pe.value_load(slot_tab[0:1, 3 * SLOTS:3 * SLOTS + 1], min_val=NE - 1, max_val=SLOTS - 2)
        turn_x(1)
        gate_up(0, 0, None)
        pe.wait_ge(xt_l, 1)
        turn_x(2)
        with pe.Fori(0, SLOTS - 2) as s:
            with pe.If(s < last):
                e = pe.value_load(slot_tab[0:1, bass.ds(s + 1, 1)], min_val=0, max_val=NE - 1)
                e_before = pe.value_load(slot_tab[0:1, bass.ds(s, 1)], min_val=0, max_val=NE - 1)
                gate_up(s + 1, e, s)
                pe.wait_ge(xt_l, s + 2)
                turn_x(s + 3)
                down(s, e_before)
        turn_hid(last)
        down(last, NE - 1)

    block_cm.__exit__(None, None, None)


def kernel(x, meta_tokens, norm_mix_g, w_in, conf_dw_w, conf_dw_b, conf_ln_g, conf_ln_b, sc_conv_w, w_out, norm_ffn_g,
           w_router_group, b_router_group, w_router_expert, b_router_expert, w_exp_gate, w_exp_up, w_exp_down,
           final_norm_g):
    import numpy as np
    import concourse.bacc as bacc
    from concourse.bass_utils import run_bass_kernel_spmd

    a = {k: np.ascontiguousarray(v) for k, v in dict(
        x=x, meta=meta_tokens, w_in=w_in, w_out=w_out, g_mix=norm_mix_g, g_ffn=norm_ffn_g, g_fin=final_norm_g,
        cw=conf_dw_w, cb=conf_dw_b, lg=conf_ln_g, lb=conf_ln_b, sw=sc_conv_w, rg=w_router_group, bg=b_router_group,
        re=w_router_expert, be=b_router_expert, wg=w_exp_gate, wu=w_exp_up, wd=w_exp_down).items()}
    parts = a["w_in"][0].reshape(KD, P, 5, NJ, P)[:, :, [1, 0, 3, 4, 2]]
    w_in_l = np.ascontiguousarray(parts.transpose(3, 2, 1, 0, 4)).reshape(NJ * ROLES, P, KD * P)
    chan = np.concatenate([a["cw"][0], a["cb"], a["lg"], a["lb"], a["sw"][0]], axis=0)
    chan = np.ascontiguousarray(chan.reshape(NCH, NJ, P).transpose(2, 1, 0)).reshape(P, NJ * NCH)
    arrays = {
        "x": a["x"][0], "meta": a["meta"], "w_in": w_in_l, "chan": chan, "g_mix": a["g_mix"][0], "w_out": a["w_out"][0],
        "g_ffn": a["g_ffn"][0],
        "w_rt": np.ascontiguousarray(np.concatenate([a["rg"][0], a["re"][0]], axis=1)),
        "b_rt": np.ascontiguousarray(np.concatenate([a["bg"][0], a["be"][0]])),
        "w_gate": a["wg"][0], "w_up": a["wu"][0], "w_down": a["wd"][0], "g_fin": a["g_fin"],
    }
    nc = bacc.Bacc("TRN2", target_bir_lowering=False, num_devices=1)
    args = [nc.dram_tensor(f"in_{k}", v.shape, mybir.dt.from_np(v.dtype), kind="ExternalInput").ap()
            for k, v in arrays.items()]
    args.append(nc.dram_tensor("out_0", (SEQ, D), F32, kind="ExternalOutput").ap())
    trunk(nc, *args)
    r = run_bass_kernel_spmd(nc, [{f"in_{k}": v for k, v in arrays.items()}], core_ids=[0])
    return r.results[0]["out_0"].reshape(1, SEQ, D)
```

```python
import concourse.bass as bass
from concourse import mybir
from concourse.alu_op_type import AluOpType as ALU

ACT = mybir.ActivationFunctionType
AX = mybir.AxisListType
F32 = mybir.dt.float32
F32R = mybir.dt.float32r
I32 = mybir.dt.int32
U32 = mybir.dt.uint32

P = 128
D = 1024
KD = D // P
META = 16
SEQ = 1024
NT = SEQ // P
TG = META + SEQ
CW = 512
NJ = CW // P
TAPS, STAPS = 31, 3
PAD = TAPS - 1 - META
ROLES = 5
GL, UU, CC, VV, BB = range(ROLES)
BLK = [(0, 348), (348, 346), (694, 346)]
NCH = TAPS + 3 + STAPS
CB, LG, LB, SW = TAPS, TAPS + 1, TAPS + 2, TAPS + 3
NG, NEG = 4, 8
NE = NG * NEG
NL = NG + NE
F = 512
KF = F // P
GUC, DNC = 8, 4
MAXB = 2 * SEQ // P
MAX_LAST = NE + MAXB - 2
SLOTS = MAX_LAST + 4
EPS = 1e-6
OOB = 4096


class Tally:

    def __init__(self, eng, sem):
        self.eng, self.sem, self.n, self.term = eng, sem, 0, None

    def value(self):
        return self.n if self.term is None else self.term + self.n

    def step(self, ins):
        ins.then_inc(self.sem, 1)
        self.n += 1
        self.eng.wait_ge(self.sem, self.value())

    def loop(self, i, per, first=0):
        self.saved, self.per, self.first = self.n, per, first
        self.term = (i - first) * per if first else i * per

    def end(self, trips):
        assert self.n - self.saved == self.per, (self.n - self.saved, self.per)
        self.n = self.saved + self.per * trips
        self.term = None


def trunk(nc, x, meta, w_in, chan, g_mix, w_out, g_ffn, w_rt, b_rt, w_gate, w_up, w_down, g_fin, out):
    hn_rows = nc.dram_tensor("hn_rows", (SEQ, D), F32).ap()
    y_rows = nc.dram_tensor("y_rows", (2 * SEQ, D), F32).ap()

    R1, R2, R3, R4, ST, SM = 0, 66560, 107520, 140288, 157056, 206208
    base0 = (nc.sbuf_base + 31) // 32 * 32

    def at(name, shape, dt, offset):
        return nc.alloc_sbuf_tensor_at(name, shape, dt, offset=base0 + offset)

    class Bump:
        def __init__(self, start, end):
            self.o, self.end = start, end

        def __call__(self, name, shape, dt=F32):
            n = 4
            for s in shape[1:]:
                n *= s
            t = at(name, shape, dt, self.o)
            self.o += (n + 31) // 32 * 32
            assert self.o <= self.end, (name, self.o, self.end)
            return t

    xn_hi = at("xn_hi", [P, KD, TG], F32R, R1)
    xn_lo = at("xn_lo", [P, KD, TG], F32R, R1 + KD * TG * 4)
    wi_hi = at("wi_hi", [P, ROLES, KD * P], F32R, R2)
    wi_lo = at("wi_lo", [P, ROLES, KD * P], F32R, R2 + ROLES * KD * P * 4)
    mix = at("mix", [P, KD, SEQ], F32, R3)
    r = Bump(R3, R4)
    x_in = r("x_in", [P, 2, D])
    x_sc = r("x_sc", [P, 2, D])
    g_mix_b = r("g_mix_b", [P, D])
    r = Bump(R4, ST)
    a_buf = r("a_buf", [P, PAD + TG])
    cv = r("cv", [P, TG])
    sig = r("sig", [P, TG])
    c_sb = r("c_sb", [P, TG])
    r = Bump(R4, ST)
    sq = r("sq", [P, 2, NJ, 512])
    wo_hi = at("wo_hi", [P, KD, D], F32R, R1)
    wo_lo = at("wo_lo", [P, KD, D], F32R, R1 + KD * D * 4)
    r = Bump(R2, R3)
    m_hi = r("m_hi", [P, 2, KD, P], F32R)
    m_lo = r("m_lo", [P, 2, KD, P], F32R)
    x_res = r("x_res", [P, 2, D])
    std = at("std", [P, 2, 512], F32, r.o)
    rstd = at("rstd", [P, 2, 512], F32, r.o + 4096)
    hn = r("hn", [P, 2, D])
    hn_t = r("hn_t", [P, KD, P])
    g_ffn_b = r("g_ffn_b", [P, D])
    r = Bump(R4, ST)
    tri = r("tri", [P, P])
    ones = r("ones", [P, P])
    iota_r = r("iota_r", [P, P])
    iota_s = r("iota_s", [P, SLOTS])
    part = r("part", [P, 1])
    part1 = r("part1", [P, 1])
    rev = r("rev", [P, NEG])
    thr = r("thr", [P, 7, NE])
    asg_id = r("asg_id", [P, 2, NT])
    a1 = r("a1", [P, NT, NG, NEG])
    a2 = r("a2", [P, NT, NG, NEG])
    a12 = r("a12", [P, NT, NE])
    before = r("before", [P, NT + 1, NE])
    pos = r("pos", [P, NT, NE])
    dest = r("dest", [P, NT, NE])
    prod = r("prod", [P, NT, NE])
    more = r("more", [P, 7, NE])
    b_sq = r("b_sq", [P, D])
    r = Bump(R2, R3)
    one_r = r("one_r", [P, 2 * NT, P], F32R)
    one_s = r("one_s", [P, 2 * NT, SLOTS])
    val_s = r("val_s", [P, 2 * NT, 3, SLOTS], F32R)
    g_sh = r("g_sh", [P, NT, NG])
    g_ex = r("g_ex", [P, NT, NG])
    g_one = r("g_one", [P, NT, NG])
    g_key = r("g_key", [P, NT, NG])
    sel = r("sel", [P, NT, NEG])
    sel2 = r("sel2", [P, NT, NEG])
    key = r("key", [P, NT, NEG])
    o1 = r("o1", [P, NT, NEG])
    o2 = r("o2", [P, NT, NEG])
    vec = r("vec", [P, 12, NT])
    wk = r("wk", [P, 2, NT])
    wk_hi = r("wk_hi", [P, 2, NT], F32R)
    wk_lo = r("wk_lo", [P, 2, NT], F32R)
    w_inv = r("w_inv", [P, SLOTS])
    dd = r("dd", [P, 2, NT])
    dd_i = r("dd_i", [P, 2, NT], I32)
    sl_i = r("sl_i", [P, 2, NT], I32)
    ro_i = r("ro_i", [P, 2, NT], I32)
    sl_f = r("sl_f", [P, 2, NT])
    ro_f = r("ro_f", [P, 2, NT])
    nblk = r("nblk", [P, NE])
    s_end = r("s_end", [P, NE])
    s_beg = r("s_beg", [P, NE])
    junk = r("junk", [P, NE])
    tab = r("tab", [P, 3])
    vm = r("vm", [P, SLOTS])
    inv = r("inv", [P, SLOTS])
    v_i = r("v_i", [P, SLOTS], I32)
    v_f = r("v_f", [P, SLOTS])
    gu_hi = at("gu_hi", [P, GUC, D], F32R, R1)
    gu_lo = at("gu_lo", [P, GUC, D], F32R, R1 + GUC * D * 4)
    dn_hi = at("dn_hi", [P, DNC, D], F32R, R2)
    dn_lo = at("dn_lo", [P, DNC, D], F32R, R2 + DNC * D * 4)
    xt_hi = at("xt_hi", [P, KD, P], F32R, R2 + 2 * DNC * D * 4)
    xt_lo = at("xt_lo", [P, KD, P], F32R, R2 + 2 * DNC * D * 4 + D * 4)
    r = Bump(R4, ST)
    ht_hi = r("ht_hi", [P, KF, P], F32R)
    ht_lo = r("ht_lo", [P, KF, P], F32R)
    x_g = r("x_g", [P, D])
    y_sb = r("y_sb", [P, D])
    hid = r("hid", [P, F])
    sil = r("sil", [P, F])
    r = Bump(R1, R3)
    ys = r("ys", [P, NT, 2, D])
    f_sq = r("f_sq", [P, D])
    g_fin_b = at("g_fin_b", [P, D], F32, R2 + 2 * DNC * D * 4)

    stage = at("stage", [P, GUC + DNC, D], F32, ST)
    r = Bump(SM, SM + 6624)
    ident = r("ident", [P, P])
    ones_cw = r("ones_cw", [P, P])
    chan_sb = r("chan_sb", [P, NJ * NCH])
    logit = r("logit", [P, NT, NL])
    w_rt_sb = r("w_rt_sb", [P, KD, NL])
    b_rt_b = r("b_rt_b", [P, NL])
    stat = r("stat", [P, 3, 32])
    eps = r("eps", [P, 1])
    gidx = r("gidx", [P, SLOTS], I32)
    sidx = r("sidx", [P, SLOTS], I32)
    wgt = r("wgt", [P, SLOTS])
    gidx_cur = r("gidx_cur", [P, 1], I32)
    sidx_cur = r("sidx_cur", [P, 1], I32)
    slot_tab = r("slot_tab", [1, 3 * SLOTS + 1], I32)

    ps = nc.alloc_psum_tensor("ps", [P, 8, 512], F32)

    def sem(name):
        return nc.alloc_semaphore(name)

    param_in = [sem(f"param_in{i}") for i in range(5)]
    g2_in = sem("g2_in")
    g3_in = sem("g3_in")
    x_full = [sem(f"x_full{i}") for i in range(2)]
    wi_full = [sem(f"wi_full{i}") for i in range(ROLES)]
    wo_full = [sem(f"wo_full{i}") for i in range(KD)]
    xr_full = [sem(f"xr_full{i}") for i in range(2)]
    hn_out = [sem(f"hn_out{i}") for i in range(2)]
    st_full = [sem(f"st_full{i}") for i in range(GUC + DNC)]
    consts = sem("consts")
    rconsts = sem("rconsts")
    pool_own = sem("pool_own")
    act_own = sem("act_own")
    dve_own = sem("dve_own")
    eps_ok = sem("eps_ok")
    meta_zero = sem("meta_zero")
    root = sem("root")
    scaled = sem("scaled")
    turned = sem("turned")
    xh_done = sem("xh_done")
    xl_done = sem("xl_done")
    wi_h = sem("wi_h")
    wi_l = sem("wi_l")
    proj = sem("proj")
    ev_act = sem("ev_act")
    ev_dve = sem("ev_dve")
    conv_done = sem("conv_done")
    mean_done = sem("mean_done")
    cent_done = sem("cent_done")
    sq_done = sem("sq_done")
    var_done = sem("var_done")
    std_done = sem("std_done")
    nrm_done = sem("nrm_done")
    silu_done = sem("silu_done")
    wo_h = sem("wo_h")
    wo_l = sem("wo_l")
    mh_done = sem("mh_done")
    ml_done = sem("ml_done")
    op_done = sem("op_done")
    h_done = sem("h_done")
    hroot = sem("hroot")
    hn_done = sem("hn_done")
    hturned = sem("hturned")
    hnt_done = sem("hnt_done")
    rt_done = sem("rt_done")
    lg_done = sem("lg_done")
    exp_in = sem("exp_in")
    exp_out = sem("exp_out")
    a_ready = sem("a_ready")
    ranks = sem("ranks")
    inv_in = sem("inv_in")
    inv_out = sem("inv_out")
    tab_in = sem("tab_in")
    tab_out = sem("tab_out")
    tables = sem("tables")
    gu_h = sem("gu_h")
    gu_l = sem("gu_l")
    dn_h = sem("dn_h")
    dn_l = sem("dn_l")
    gu_used = sem("gu_used")
    dn_used = sem("dn_used")
    idx_ok = sem("idx_ok")
    xg_zero = sem("xg_zero")
    gathered = sem("gathered")
    xt_done = sem("xt_done")
    xt_h = sem("xt_h")
    xt_l = sem("xt_l")
    sil_done = sem("sil_done")
    hid_done = sem("hid_done")
    ht_done = sem("ht_done")
    ht_h = sem("ht_h")
    ht_l = sem("ht_l")
    y_ev = sem("y_ev")
    y_out = sem("y_out")
    ys_full = [sem(f"ys_full{i}") for i in range(NT)]
    z_done = sem("z_done")
    froot = sem("froot")
    o_done = sem("o_done")
    o_out = [sem(f"o_out{i}") for i in range(2)]

    WO_SLOT = [5, 6, 7, 8, 9, 10, 11, 0]
    A0C, BC, FC = 0, 9, 17

    def rows(t):
        return mix[:, :, bass.ds(t * P, P)] if not isinstance(t, int) else mix[:, :, t * P:(t + 1) * P]

    def half(h):
        return slice(512 * h, 512 * h + 512)

    def split8(ap):
        return ap.rearrange("p (k c) -> p k c", c=P)

    block_cm = nc.Block()
    block = block_cm.__enter__()

    @block.sync
    def _(sp):
        sp.wait_ge(meta_zero, 1)
        sp.dma_start(x_in[0:META, 0, :], meta).then_inc(x_full[0], 16)
        sp.dma_start(x_in[:, 1, :], x[0:P, :]).then_inc(x_full[1], 16)
        sp.dma_start(g_mix_b[:], g_mix.partition_broadcast(P)).then_inc(param_in[0], 16)
        for q in (GL, UU):
            sp.dma_start(stage[:, q, :], w_in[q]).then_inc(wi_full[q], 16)
        sp.dma_start(chan_sb[:], chan).then_inc(param_in[1], 16)
        with sp.Fori(0, 3) as i:
            for half in range(2):
                sp.wait_ge(scaled, 2 * i + half + 1)
                sp.dma_start(x_in[:, half, :], x[bass.ds((2 * i + half + 1) * P, P), :]).then_inc(x_full[half], 16)
        sp.wait_ge(scaled, 7)
        sp.dma_start(x_in[:, 0, :], x[7 * P:8 * P, :]).then_inc(x_full[0], 16)
        for q in (CC, VV, BB):
            sp.dma_start(stage[:, q, :], w_in[q]).then_inc(wi_full[q], 16)
        for k in range(KD - 1):
            sp.dma_start(stage[:, WO_SLOT[k], :], w_out[k * P:(k + 1) * P, :]).then_inc(wo_full[k], 16)
        sp.dma_start(w_rt_sb[:], w_rt.rearrange("(k p) n -> p k n", p=P)).then_inc(param_in[2], 16)
        sp.dma_start(b_rt_b[:], b_rt.partition_broadcast(P)).then_inc(param_in[3], 16)
        with sp.Fori(0, NJ - 1) as j:
            for q in range(ROLES):
                sp.wait_ge(wi_l, ROLES * j + q + 1)
                sp.dma_start(stage[:, q, :], w_in[bass.ds(ROLES * j + ROLES + q, 1)].rearrange("a p n -> (a p) n")).then_inc(wi_full[q], 16)
        sp.wait_ge(wi_l, ROLES * NJ)
        sp.dma_start(stage[:, WO_SLOT[7], :], w_out[7 * P:8 * P, :]).then_inc(wo_full[7], 16)
        sp.wait_ge(proj, NJ * ROLES * 3)
        sp.dma_start(g_ffn_b[:], g_ffn.partition_broadcast(P)).then_inc(g2_in, 16)
        for t in range(2):
            sp.dma_start(x_res[:, t, :], x[t * P:(t + 1) * P, :]).then_inc(xr_full[t], 16)

        def load_expert(e, first, n, waits):
            for c in range(first, first + n):
                if waits is not None:
                    s, v = waits
                    sp.wait_ge(s, v + (c - first) + 1)
                if c < GUC:
                    src, q = (w_up if c % 2 else w_gate), c // 2
                    ap = src[e].rearrange("(p k) f -> p (k f)", k=KD)[:, q * D:(q + 1) * D] if isinstance(e, int) else \
                        src[bass.ds(e, 1)].rearrange("a (p k) f -> (a p) (k f)", k=KD)[:, q * D:(q + 1) * D]
                else:
                    q = c - GUC
                    ap = w_down[e].rearrange("(p k) d -> p (k d)", k=KF)[:, q * D:(q + 1) * D] if isinstance(e, int) else \
                        w_down[bass.ds(e, 1)].rearrange("a (p k) d -> (a p) (k d)", k=KF)[:, q * D:(q + 1) * D]
                sp.dma_start(stage[:, c, :], ap).then_inc(st_full[c], 16)

        sp.wait_ge(wo_l, KD)
        load_expert(0, 0, GUC + DNC, None)
        with sp.Fori(0, 3) as i:
            for par in range(2):
                sp.wait_ge(hn_done, 2 * i + par + 1)
                sp.dma_start(hn_rows[bass.ds((2 * i + par) * P, P), :], hn[:, par, :]).then_inc(hn_out[par], 16)
                sp.dma_start(x_res[:, par, :], x[bass.ds((2 * i + par + 2) * P, P), :]).then_inc(xr_full[par], 16)
        for t in (6, 7):
            sp.wait_ge(hn_done, t + 1)
            sp.dma_start(hn_rows[t * P:(t + 1) * P, :], hn[:, t % 2, :]).then_inc(hn_out[t % 2], 16)
        load_expert(1, 0, GUC, (gu_l, 0))
        with sp.Fori(0, NE - 2) as e:
            load_expert(e + 2, 0, GUC, (gu_l, e * GUC + GUC))
            load_expert(e + 1, GUC, DNC, (dn_l, e * DNC))
        load_expert(NE - 1, GUC, DNC, (dn_l, DNC * (NE - 2)))
        sp.wait_ge(tables, 1)
        last = sp.value_load(slot_tab[0:1, 3 * SLOTS:3 * SLOTS + 1], min_val=NE - 1, max_val=MAX_LAST)
        sp.wait_ge(xt_l, last + 2)
        sp.wait_ge(gu_used, last * GUC + GUC)
        sp.dma_start(g_fin_b[:], g_fin.partition_broadcast(P)).then_inc(g3_in, 16)
        sp.wait_ge(y_out, last * 16 + 16)
        for t in range(NT):
            for k in range(2):
                sp.dma_start(ys[:, t, k, :], y_rows[k * SEQ + t * P:k * SEQ + (t + 1) * P, :]).then_inc(ys_full[t], 16)
        for t in range(NT):
            sp.wait_ge(o_done, t + 1)
            sp.dma_start(out[t * P:(t + 1) * P, :], ys[:, t, 1, :]).then_inc(o_out[t % 2], 16)
        for h in range(2):
            sp.wait_ge(o_out[h], 16 * NT // 2)

    @block.gpsimd
    def _(pool):
        own = Tally(pool, pool_own)
        nc.gpsimd.memset(x_in[:, 0, :], 0.0).then_inc(meta_zero, 1)
        own.step(nc.gpsimd.memset(ident[:], 0.0))
        nc.gpsimd.affine_select(out=ident[:], in_=ident[:], compare_op=ALU.not_equal, fill=1.0, base=0,
                                pattern=[[-1, P]], channel_multiplier=1).then_inc(consts, 1)
        nc.gpsimd.memset(ones_cw[:], 1.0 / CW).then_inc(consts, 1)
        for k in range(KD):
            pool.wait_ge(wo_h, k + 1)
            nc.gpsimd.tensor_tensor(wo_lo[:, k, :], stage[:, WO_SLOT[k], :], wo_hi[:, k, :].bitcast(F32),
                                    ALU.subtract).then_inc(wo_l, 1)
        pool.wait_ge(var_done, 2)
        nc.gpsimd.memset(ones[:], 1.0).then_inc(rconsts, 1)
        own.step(nc.gpsimd.memset(tri[:], 1.0))
        nc.gpsimd.affine_select(out=tri[:], in_=tri[:], compare_op=ALU.is_gt, fill=0.0, base=0,
                                pattern=[[1, P]], channel_multiplier=-1).then_inc(rconsts, 1)
        for ap, pattern, base, cm in (
                (iota_r[:], [[1, P]], 0, 0), (iota_s[:], [[1, SLOTS]], 0, 0), (part[:], [[0, 1]], 0, 1),
                (part1[:], [[0, 1]], 1, 1), (rev[:], [[-1, NEG]], NEG, 0), (thr[:], [[P, 7], [0, NE]], P, 0),
                (asg_id[:], [[SEQ, 2], [P, NT]], 1, 1)):
            nc.gpsimd.iota(ap, pattern=pattern, base=base, channel_multiplier=cm,
                           allow_small_or_imprecise_dtypes=True).then_inc(rconsts, 1)

        for c in range(GUC):
            pool.wait_ge(gu_h, c + 1)
            nc.gpsimd.tensor_tensor(gu_lo[:, c, :], stage[:, c, :], gu_hi[:, c, :].bitcast(F32), ALU.subtract).then_inc(gu_l, 1)

        pool.wait_ge(tables, 1)
        for h in range(2):
            pool.wait_ge(hn_out[h], 16 * NT // 2)
        nc.gpsimd.memset(x_g[:], 0.0).then_inc(xg_zero, 1)
        last = pool.value_load(slot_tab[0:1, 3 * SLOTS:3 * SLOTS + 1], min_val=NE - 1, max_val=MAX_LAST)

        pool.wait_ge(xg_zero, 1)
        def column(table, g):
            return table[:, g:g + 1] if isinstance(g, int) else table[:, bass.ds(g, 1)]

        def gather(g, copies):
            if not isinstance(g, int) or g:
                pool.wait_ge(xt_done, g)
            nc.gpsimd.tensor_copy(gidx_cur[:], column(gidx, g)).then_inc(idx_ok, 1)
            pool.wait_ge(idx_ok, copies)
            nc.gpsimd.indirect_dma_start(out=x_g[:], out_offset=None, in_=hn_rows,
                                         in_offset=bass.IndirectOffsetOnAxis(ap=gidx_cur[:, 0:1].bitcast(U32), axis=0),
                                         bounds_check=g + SEQ - 1, oob_is_err=False).then_inc(gathered, 16)

        def scatter(g, copies):
            if not isinstance(g, int) or g:
                pool.wait_ge(y_out, g * 16)
            nc.gpsimd.tensor_copy(sidx_cur[:], column(sidx, g)).then_inc(idx_ok, 1)
            pool.wait_ge(idx_ok, copies)
            pool.wait_ge(y_ev, g + 1)
            nc.gpsimd.indirect_dma_start(out=y_rows,
                                         out_offset=bass.IndirectOffsetOnAxis(ap=sidx_cur[:, 0:1].bitcast(U32), axis=0),
                                         in_=y_sb[:], in_offset=None,
                                         bounds_check=g + 2 * SEQ - 1, oob_is_err=False).then_inc(y_out, 16)

        for g in range(3):
            gather(g, g + 1)
        gather(3, 4)
        scatter(0, 5)
        with pool.Fori(1, MAX_LAST) as i:
            with pool.If(i < last):
                gather(i + 3, 2 * i + 4)
                scatter(i, 2 * i + 5)
        scatter(last, 2 * last + 4)

    @block.scalar
    def _(act):
        own = Tally(act, act_own)
        act.wait_ge(eps_ok, 1)

        def mean_root(src, junk_out, column, done):
            ssq = stat[:, 0, bass.ds(column, 1)] if not isinstance(column, int) else stat[:, 0, column:column + 1]
            rt = stat[:, 1, bass.ds(column, 1)] if not isinstance(column, int) else stat[:, 1, column:column + 1]
            own.step(nc.scalar.activation(junk_out, src, ACT.Square, accum_out=ssq))
            nc.scalar.activation(rt, ssq, ACT.Sqrt, bias=eps[:], scale=1.0 / D).then_inc(done, 1)

        def a0_root(n, half):
            if not isinstance(n, int) or n >= 2:
                act.wait_ge(turned, n - 1)
            act.wait_ge(x_full[half], 16 * ((n + (2 - half)) // 2) if isinstance(n, int) else n)
            mean_root(x_in[:, half, :], x_sc[:, half, :], n, root)

        def a0_hi(n, half, t0, w):
            act.wait_ge(turned, n + 1)
            for b in range(2):
                src = ps[:, 2 * half + b, :].rearrange("p (k c) -> p k c", c=P)[:, :, 0:w]
                o = xn_hi[:, 4 * b:4 * b + 4, t0:t0 + w] if isinstance(t0, int) else xn_hi[:, 4 * b:4 * b + 4, bass.ds(t0, w)]
                ins = nc.scalar.copy(o, src)
            ins.then_inc(xh_done, 1)

        def wi_split(q, full):
            act.wait_ge(wi_full[q], full)
            nc.scalar.copy(wi_hi[:, q, :], stage[:, q, :]).then_inc(wi_h, 1)

        a0_root(0, 0)
        wi_split(GL, 16)
        wi_split(UU, 16)
        act.wait_ge(x_full[1], 16)
        mean_root(x_in[:, 1, :], x_sc[:, 1, :], 1, root)
        a0_hi(0, 0, 0, META)
        with act.Fori(0, 3) as i:
            own.loop(i, 2)
            for h in range(2):
                act.wait_ge(turned, 2 * i + h + 1)
                act.wait_ge(x_full[h], 16 * i + 32)
                mean_root(x_in[:, h, :], x_sc[:, h, :], 2 * i + 2 + h, root)
                a0_hi(2 * i + 1 + h, 1 - h, (2 * i + h) * P + META, P)
            own.end(3)
        act.wait_ge(turned, 7)
        act.wait_ge(x_full[0], 16 * 5)
        mean_root(x_in[:, 0, :], x_sc[:, 0, :], 8, root)
        a0_hi(7, 1, 6 * P + META, P)
        a0_hi(8, 0, 7 * P + META, P)
        for q in (CC, VV, BB):
            wi_split(q, 16)

        def body_a(j, split_next):
            for b, (t0, n) in enumerate(BLK):
                act.wait_ge(proj, 15 * j + b + 1)
                nc.scalar.activation(sig[:, t0:t0 + n], ps[:, b, 0:n], ACT.Sigmoid).then_inc(ev_act, 1)
            if split_next:
                wi_split(GL, 16 * j + 32)
                act.wait_ge(proj, 15 * j + 6)
                wi_split(UU, 16 * j + 32)
            for b, (t0, n) in enumerate(BLK):
                act.wait_ge(proj, 15 * j + 6 + b + 1)
                nc.scalar.copy(c_sb[:, t0:t0 + n], ps[:, b, 0:n]).then_inc(ev_act, 1)
            if split_next:
                wi_split(CC, 16 * j + 32)
                act.wait_ge(proj, 15 * j + 12)
                wi_split(VV, 16 * j + 32)
                act.wait_ge(proj, 15 * j + 15)
                wi_split(BB, 16 * j + 32)

        with act.Fori(0, NJ - 1) as j:
            body_a(j, True)
        body_a(NJ - 1, False)
        act.wait_ge(proj, NJ * 15)
        for k in range(KD):
            act.wait_ge(wo_full[k], 16)
            nc.scalar.copy(wo_hi[:, k, :], stage[:, WO_SLOT[k], :]).then_inc(wo_h, 1)

        def m_split(t, par):
            if not isinstance(t, int) or t >= 2:
                act.wait_ge(op_done, t - 1)
            nc.scalar.copy(m_hi[:, par], rows(t)).then_inc(mh_done, 1)

        def squares(h):
            act.wait_ge(cent_done, h + 1)
            for j in range(NJ):
                nc.scalar.activation(sq[:, h, j, :], mix[:, j, half(h)], ACT.Square).then_inc(sq_done, 1)

        def deviation(h):
            act.wait_ge(var_done, h + 1)
            nc.scalar.activation(std[:, h, :], ps[:, 6 + h, :], ACT.Sqrt, bias=eps[:]).then_inc(std_done, 1)

        def ln_silu(h):
            act.wait_ge(nrm_done, h + 1)
            for j in range(NJ):
                c = j * NCH
                ins = nc.scalar.activation(mix[:, j, half(h)], mix[:, j, half(h)], ACT.Silu,
                                           bias=chan_sb[:, c + LB:c + LB + 1], scale=chan_sb[:, c + LG:c + LG + 1])
            ins.then_inc(silu_done, 1)
            act.wait_ge(silu_done, h + 1)

        squares(0)
        squares(1)
        deviation(0)
        deviation(1)
        ln_silu(0)
        act.wait_ge(ev_dve, 3 + 9 * NJ)

        m_split(0, 0)
        m_split(1, 1)
        ln_silu(1)

        def b_root(t):
            act.wait_ge(h_done, t + 1)
            mean_root(rows(t), split8(b_sq[:]), t + BC, hroot)

        def hnt_copy(t):
            act.wait_ge(hturned, t + 1)
            for b in range(2):
                ins = nc.scalar.copy(hn_t[:, 4 * b:4 * b + 4, :], split8(ps[:, 4 + b, :]))
            ins.then_inc(hnt_done, 1)

        b_root(0)
        with act.Fori(0, 3) as i:
            own.loop(i, 2)
            for k in range(2):
                m_split(2 * i + 2 + k, k)
                hnt_copy(2 * i + k)
                b_root(2 * i + 1 + k)
            own.end(3)
        hnt_copy(6)
        b_root(7)
        hnt_copy(7)

        act.wait_ge(exp_in, 1)
        nc.scalar.activation(g_ex[:], g_sh[:], ACT.Exp).then_inc(exp_out, 1)
        act.wait_ge(exp_in, 2)
        nc.scalar.activation(vec[:, 5, :], vec[:, 4, :], ACT.Exp).then_inc(exp_out, 1)

        def gu_split(e1, c, used):
            if used is not None:
                act.wait_ge(gu_used, used + c + 1)
            act.wait_ge(st_full[c], e1 * 16 + 16)
            nc.scalar.copy(gu_hi[:, c, :], stage[:, c, :]).then_inc(gu_h, 1)

        def xt_copy(count):
            act.wait_ge(xt_done, count)
            for b in range(2):
                ins = nc.scalar.copy(xt_hi[:, 4 * b:4 * b + 4, :], ps[:, 4 + b, :].rearrange("p (k c) -> p k c", c=P))
            ins.then_inc(xt_h, 1)

        def ht_copy(s):
            act.wait_ge(ht_done, s + 1)
            nc.scalar.copy(ht_hi[:], ps[:, 6, :].rearrange("p (k c) -> p k c", c=P)).then_inc(ht_h, 1)

        def y_copy(s, copies):
            act.wait_ge(dn_used, s * DNC + DNC)
            act.wait_ge(idx_ok, copies)
            for n in range(2):
                ins = nc.scalar.activation(y_sb[:, 512 * n:512 * n + 512], ps[:, 2 + n, :], ACT.Copy,
                                           scale=wgt[:, bass.ds(s, 1)])
            ins.then_inc(y_ev, 1)

        act.wait_ge(op_done, NT)
        for c in range(GUC):
            gu_split(0, c, None)
        act.wait_ge(tables, 1)
        last = act.value_load(slot_tab[0:1, 3 * SLOTS:3 * SLOTS + 1], min_val=NE - 1, max_val=MAX_LAST)

        def body_c(s, first_step):
            g = 0 if first_step else s + 1
            e = act.value_load(slot_tab[0:1, bass.ds(g, 1)], min_val=0, max_val=NE - 1) if not first_step else 0
            beg = act.value_load(slot_tab[0:1, bass.ds(g + SLOTS, 1)], min_val=0, max_val=1) if not first_step else 1
            end = act.value_load(slot_tab[0:1, bass.ds(g + 2 * SLOTS, 1)] if not first_step else
                                 slot_tab[0:1, 2 * SLOTS:2 * SLOTS + 1], min_val=0, max_val=1)
            with act.If(end > 0):
                for c in range(GUC):
                    gu_split(e + 1, c, g * GUC)
                    if c == 3 and not first_step:
                        ht_copy(s)
            with act.Else():
                if not first_step:
                    ht_copy(s)
                else:
                    act.wait_ge(gu_used, 1)
            act.wait_ge(gu_used, g * GUC + GUC)
            nc.scalar.activation(sil[:], ps[:, 0, :], ACT.Silu).then_inc(sil_done, 1)
            xt_copy(g + 2)
            def dn_split():
                for c in range(DNC):
                    if not first_step:
                        act.wait_ge(dn_used, s * DNC + c + 1)
                    act.wait_ge(st_full[GUC + c], e * 16 + 16)
                    nc.scalar.copy(dn_hi[:, c, :], stage[:, GUC + c, :]).then_inc(dn_h, 1)
            if first_step:
                dn_split()
            else:
                with act.If(beg > 0):
                    dn_split()
                y_copy(s, 2 * s + 5)

        xt_copy(1)
        body_c(None, True)
        with act.Fori(0, MAX_LAST) as s:
            with act.If(s < last):
                body_c(s, False)
        ht_copy(last)
        y_copy(last, 2 * last + 4)

        for t in range(NT):
            act.wait_ge(z_done, t + 1)
            own.step(nc.scalar.activation(f_sq[:], ys[:, t, 0, :], ACT.Square, accum_out=stat[:, 0, FC + t:FC + t + 1]))
            nc.scalar.activation(stat[:, 1, FC + t:FC + t + 1], stat[:, 0, FC + t:FC + t + 1], ACT.Sqrt, bias=eps[:],
                                 scale=1.0 / D).then_inc(froot, 1)

    @block.vector
    def _(dve):
        own = Tally(dve, dve_own)
        v = nc.vector
        v.memset(eps[:], EPS).then_inc(eps_ok, 1)
        v.memset(a_buf[:, 0:PAD], 0.0).then_inc(ev_dve, 3)

        def a0_scale(n, half):
            col = (lambda k: stat[:, k, bass.ds(n, 1)]) if not isinstance(n, int) else (lambda k: stat[:, k, n:n + 1])
            dve.wait_ge(root, n + 1)
            own.step(v.reciprocal(col(2), col(1)))
            v.scalar_tensor_tensor(out=x_sc[:, half, :], in0=x_in[:, half, :], scalar=col(2), in1=g_mix_b[:],
                                   op0=ALU.mult, op1=ALU.mult).then_inc(scaled, 1)

        def a0_lo(n, half, t0, w):
            dve.wait_ge(xh_done, n + 1)
            for b in range(2):
                src = ps[:, 2 * half + b, :].rearrange("p (k c) -> p k c", c=P)[:, :, 0:w]
                if isinstance(t0, int):
                    hi, lo = (a[:, 4 * b:4 * b + 4, t0:t0 + w] for a in (xn_hi, xn_lo))
                else:
                    hi, lo = (a[:, 4 * b:4 * b + 4, bass.ds(t0, w)] for a in (xn_hi, xn_lo))
                ins = v.tensor_tensor(lo, src, hi.bitcast(F32), ALU.subtract)
            ins.then_inc(xl_done, 1)

        def wi_low(q, count):
            dve.wait_ge(wi_h, count)
            v.tensor_tensor(wi_lo[:, q, :], stage[:, q, :], wi_hi[:, q, :].bitcast(F32), ALU.subtract).then_inc(wi_l, 1)

        dve.wait_ge(param_in[0], 16)
        a0_scale(0, 0)
        wi_low(GL, 1)
        wi_low(UU, 2)
        a0_scale(1, 1)
        a0_lo(0, 0, 0, META)
        with dve.Fori(0, 3) as i:
            own.loop(i, 2)
            for h in range(2):
                a0_scale(2 * i + 2 + h, h)
                a0_lo(2 * i + 1 + h, 1 - h, (2 * i + h) * P + META, P)
            own.end(3)
        a0_scale(8, 0)
        a0_lo(7, 1, 6 * P + META, P)
        a0_lo(8, 0, 7 * P + META, P)
        for q in (CC, VV, BB):
            wi_low(q, q + 1)
        dve.wait_ge(param_in[1], 16)

        def body_a(j, split_next):
            def const(k):
                return chan_sb[:, bass.ds(j * NCH + k, 1)] if not isinstance(j, int) else chan_sb[:, j * NCH + k:j * NCH + k + 1]

            def line(off):
                if isinstance(j, int):
                    return mix[:, off + j, :]
                return mix[:, bass.ds(j + off, 1), :].rearrange("p a t -> p (a t)")

            def taps(lo, hi):
                y = line(0)
                for k in range(lo, hi):
                    src = a_buf[:, k:k + SEQ]
                    if k == 0:
                        ins = v.tensor_scalar(y, src, const(0), const(CB), ALU.mult, ALU.add)
                    else:
                        ins = v.scalar_tensor_tensor(out=y, in0=src, scalar=const(k), in1=y, op0=ALU.mult, op1=ALU.add)
                    if k == TAPS - 1:
                        ins.then_inc(conv_done, 1)
                        dve.wait_ge(conv_done, j + 1)
                    else:
                        own.step(ins)

            def low(q):
                if split_next:
                    wi_low(q, ROLES * j + ROLES + q + 1)

            low(GL)
            for b, (t0, n) in enumerate(BLK):
                dve.wait_ge(ev_act, 6 * j + b + 1)
                dve.wait_ge(proj, 15 * j + 3 + b + 1)
                v.tensor_tensor(a_buf[:, PAD + t0:PAD + t0 + n], ps[:, 3 + b, 0:n], sig[:, t0:t0 + n],
                                ALU.mult).then_inc(ev_dve, 1)
            low(UU)
            dve.wait_ge(ev_dve, 9 * j + 6)
            taps(0, 6)
            low(CC)
            taps(6, 11)
            for b, (t0, n) in enumerate(BLK):
                dve.wait_ge(ev_act, 6 * j + 3 + b + 1)
                dve.wait_ge(proj, 15 * j + 9 + b + 1)
                v.tensor_tensor(cv[:, t0:t0 + n], ps[:, 3 + b, 0:n], c_sb[:, t0:t0 + n], ALU.mult).then_inc(ev_dve, 1)
            low(VV)
            dve.wait_ge(ev_dve, 9 * j + 9)
            s = line(NJ)
            for k in range(STAPS):
                src = cv[:, META - STAPS + 1 + k:META - STAPS + 1 + k + SEQ]
                if k == 0:
                    own.step(v.tensor_scalar(s, src, const(SW), None, ALU.mult))
                else:
                    own.step(v.scalar_tensor_tensor(out=s, in0=src, scalar=const(SW + k), in1=s, op0=ALU.mult, op1=ALU.add))
            taps(11, 13)
            for b, (t0, n) in enumerate(BLK):
                dve.wait_ge(proj, 15 * j + 12 + b + 1)
                skip = META if b == 0 else 0
                o = t0 + skip - META
                if isinstance(j, int):
                    seg = mix[:, NJ + j, o:o + n - skip]
                else:
                    seg = mix[:, bass.ds(j + NJ, 1), o:o + n - skip].rearrange("p a t -> p (a t)")
                v.tensor_tensor(seg, ps[:, b, skip:n], seg, ALU.mult).then_inc(ev_dve, 1)
            low(BB)
            taps(13, TAPS)

        with dve.Fori(0, NJ - 1) as j:
            own.loop(j, TAPS - 1 + STAPS)
            body_a(j, True)
            own.end(NJ - 1)
        body_a(NJ - 1, False)

        def center(h):
            dve.wait_ge(mean_done, h + 1)
            for j in range(NJ):
                ins = v.tensor_tensor(mix[:, j, half(h)], mix[:, j, half(h)], ps[:, 4 + h, :], ALU.subtract)
            ins.then_inc(cent_done, 1)

        def normalise(h):
            dve.wait_ge(std_done, h + 1)
            own.step(v.reciprocal(rstd[:, h, :], std[:, h, :]))
            dve.wait_ge(sq_done, NJ * (h + 1))
            for j in range(NJ):
                ins = v.tensor_tensor(mix[:, j, half(h)], mix[:, j, half(h)], rstd[:, h, :], ALU.mult)
            ins.then_inc(nrm_done, 1)
            dve.wait_ge(nrm_done, h + 1)

        center(0)
        center(1)
        normalise(0)
        normalise(1)

        def m_low(t, par):
            dve.wait_ge(mh_done, t + 1)
            v.tensor_tensor(m_lo[:, par], rows(t), m_hi[:, par].bitcast(F32), ALU.subtract).then_inc(ml_done, 1)

        def h_rows(t, par, full):
            dve.wait_ge(xr_full[par], full)
            dve.wait_ge(op_done, t + 1)
            hs = rows(t)
            for b in range(2):
                ins = v.tensor_tensor(hs[:, 4 * b:4 * b + 4, :], split8(ps[:, 2 * par + b, :]),
                                      split8(x_res[:, par, 512 * b:512 * b + 512]), ALU.add)
            ins.then_inc(h_done, 1)

        def hn_rows_of(t, par, stored):
            col = (lambda k: stat[:, k, bass.ds(t + BC, 1)]) if not isinstance(t, int) else (lambda k: stat[:, k, BC + t:BC + t + 1])
            dve.wait_ge(hroot, t + 1)
            if stored is not None:
                dve.wait_ge(hn_out[par], stored)
            own.step(v.reciprocal(col(2), col(1)))
            v.scalar_tensor_tensor(out=hn[:, par, :], in0=rows(t), scalar=col(2), in1=g_ffn_b[:],
                                   op0=ALU.mult, op1=ALU.mult).then_inc(hn_done, 1)

        def logits(t, par):
            dve.wait_ge(rt_done, t + 1)
            o = logit[:, bass.ds(t, 1), :].rearrange("p a n -> p (a n)") if not isinstance(t, int) else logit[:, t, :]
            v.tensor_tensor(o, ps[:, 6 + par, 0:NL], b_rt_b[:], ALU.add).then_inc(lg_done, 1)

        dve.wait_ge(g2_in, 16)
        dve.wait_ge(param_in[3], 16)
        m_low(0, 0)
        m_low(1, 1)
        h_rows(0, 0, 16)
        hn_rows_of(0, 0, None)
        m_low(2, 0)
        h_rows(1, 1, 16)
        hn_rows_of(1, 1, None)
        m_low(3, 1)
        logits(0, 0)
        h_rows(2, 0, 32)
        hn_rows_of(2, 0, 16)
        with dve.Fori(0, 2) as i:
            own.loop(i, 2)
            for k in range(2):
                m_low(2 * i + 4 + k, k)
                logits(2 * i + 1 + k, 1 - k)
                h_rows(2 * i + 3 + k, 1 - k, 16 * i + 32 + 16 * k)
                hn_rows_of(2 * i + 3 + k, 1 - k, 16 * i + 16 + 16 * k)
            own.end(2)
        logits(5, 1)
        h_rows(7, 1, 64)
        hn_rows_of(7, 1, 48)
        logits(6, 0)
        logits(7, 1)
        dve.wait_ge(lg_done, NT)

        dve.wait_ge(rconsts, 9)
        step = own.step
        lg_g = logit[:, :, 0:NG]
        lg_e = logit[:, :, NG:NL].rearrange("p t (g e) -> p t g e", g=NG)

        def spread(ap, n):
            return ap.unsqueeze(2).broadcast_to([P, ap.shape[1], n])

        def over_tiles(ap, n=NT):
            return ap.unsqueeze(1).broadcast_to([P, n, ap.shape[1]])

        m_g, m_1, m_2, k_m, diff, q_e, g_sum, g_top, den, r_den = (vec[:, k, :] for k in range(10))
        step(v.tensor_reduce(m_g, lg_g, AX.X, ALU.max))
        v.tensor_tensor(g_sh[:], lg_g, spread(m_g, NG), ALU.subtract).then_inc(exp_in, 1)

        def first_max(src, top, n, keybuf, onehot):
            step(v.tensor_tensor(keybuf, src, spread(top, n), ALU.is_equal))
            step(v.tensor_tensor(keybuf, keybuf, over_tiles(rev[:, NEG - n:NEG]), ALU.mult))
            step(v.tensor_reduce(k_m, keybuf, AX.X, ALU.max))
            step(v.tensor_tensor(onehot, keybuf, spread(k_m, n), ALU.is_equal))

        first_max(lg_g, m_g, NG, g_key[:], g_one[:])
        one4 = g_one[:].unsqueeze(3).broadcast_to([P, NT, NG, NEG])
        step(v.tensor_tensor(a1[:], lg_e, one4, ALU.mult))
        step(v.tensor_reduce(sel[:], a1[:].rearrange("p t g e -> p t e g"), AX.X, ALU.add))
        step(v.tensor_reduce(m_1, sel[:], AX.X, ALU.max))
        first_max(sel[:], m_1, NEG, key[:], o1[:])
        step(v.scalar_tensor_tensor(out=sel2[:], in0=o1[:], scalar=-3.0e38, in1=sel[:], op0=ALU.mult, op1=ALU.add))
        step(v.tensor_reduce(m_2, sel2[:], AX.X, ALU.max))
        v.tensor_tensor(diff, m_2, m_1, ALU.subtract).then_inc(exp_in, 1)
        first_max(sel2[:], m_2, NEG, key[:], o2[:])
        for a, o in ((a1, o1), (a2, o2)):
            step(v.tensor_tensor(a[:], o[:].unsqueeze(2).broadcast_to([P, NT, NG, NEG]), one4, ALU.mult))
        flat1, flat2 = (a[:].rearrange("p t g e -> p t (g e)") for a in (a1, a2))
        v.tensor_tensor(a12[:], flat1, flat2, ALU.add).then_inc(a_ready, 1)
        dve.wait_ge(exp_out, 2)
        step(v.tensor_reduce(g_sum, g_ex[:], AX.X, ALU.add))
        step(v.reciprocal(g_top, g_sum))
        step(v.tensor_scalar(den, q_e, 1.0, None, ALU.add))
        step(v.reciprocal(r_den, den))
        step(v.tensor_tensor(wk[:, 0, :], g_top, r_den, ALU.mult))
        step(v.tensor_tensor(wk[:, 1, :], wk[:, 0, :], q_e, ALU.mult))
        step(v.tensor_copy(wk_hi[:], wk[:]))
        step(v.tensor_tensor(wk_lo[:], wk[:], wk_hi[:].bitcast(F32), ALU.subtract))
        step(v.memset(before[:, 0, :], 0.0))
        dve.wait_ge(ranks, 1)
        tot = ps[:, 7, 256:512].rearrange("p (t e) -> p t e", e=NE)
        for t in range(NT):
            step(v.tensor_tensor(before[:, t + 1, :], tot[:, t, :], before[:, t, :], ALU.add))
        step(v.tensor_tensor(pos[:], ps[:, 7, 0:256].rearrange("p (t e) -> p t e", e=NE), before[:, 0:NT, :], ALU.add))
        step(v.tensor_tensor(more[:], over_tiles(before[:, NT, :], 7), thr[:], ALU.is_gt))
        step(v.tensor_reduce(nblk[:], more[:].rearrange("p b e -> p e b"), AX.X, ALU.add))
        step(v.tensor_scalar(nblk[:], nblk[:], 1.0, None, ALU.add))
        step(v.tensor_tensor_scan(s_end[:], ones[:, 0:NE], nblk[:], 0.0, ALU.mult, ALU.add))
        step(v.tensor_tensor(s_beg[:], s_end[:], nblk[:], ALU.subtract))
        step(v.tensor_scalar(junk[:], s_end[:], part[:], 0.0, ALU.is_le, ALU.add, accum_out=tab[:, 0:1]))
        step(v.tensor_scalar(junk[:], s_beg[:], part[:], 0.0, ALU.is_equal, ALU.add, accum_out=tab[:, 1:2]))
        step(v.tensor_scalar(junk[:, 0:NE - 1], s_end[:, 0:NE - 1], part1[:], 0.0, ALU.is_equal, ALU.add, accum_out=tab[:, 2:3]))
        step(v.tensor_scalar(tab[:, 0:1], tab[:, 0:1], float(NE - 1), None, ALU.min))
        v.tensor_scalar(slot_tab[0:1, 3 * SLOTS:3 * SLOTS + 1], s_end[0:1, NE - 1:NE], -1.0, None, ALU.add).then_inc(tab_in, 1)
        step(v.scalar_tensor_tensor(out=dest[:], in0=over_tiles(s_beg[:]), scalar=float(P), in1=pos[:],
                                    op0=ALU.mult, op1=ALU.add))
        for k, a in enumerate((flat1, flat2)):
            step(v.tensor_tensor(prod[:], dest[:], a, ALU.mult))
            step(v.tensor_reduce(dd[:, k, :], prod[:], AX.X, ALU.add))
        step(v.tensor_copy(dd_i[:], dd[:]))
        step(v.tensor_scalar(sl_i[:], dd_i[:], 7, None, ALU.arith_shift_right))
        step(v.tensor_scalar(ro_i[:], dd_i[:], P - 1, None, ALU.bitwise_and))
        step(v.tensor_copy(sl_f[:], sl_i[:]))
        step(v.tensor_copy(ro_f[:], ro_i[:]))
        v.tensor_tensor(one_r[:], over_tiles(iota_r[:], 2 * NT), spread(ro_f[:].rearrange("p k t -> p (k t)"), P), ALU.is_equal).then_inc(inv_in, 1)
        step(v.tensor_tensor(one_s[:], over_tiles(iota_s[:], 2 * NT), spread(sl_f[:].rearrange("p k t -> p (k t)"), SLOTS), ALU.is_equal))
        for k, a in enumerate((asg_id, wk_hi, wk_lo)):
            v.tensor_tensor(val_s[:, :, k, :], one_s[:], spread(a[:].bitcast(F32).rearrange("p k t -> p (k t)"), SLOTS),
                            ALU.mult).then_inc(inv_in, 1)
        for h in range(2):
            dve.wait_ge(hn_out[h], 16 * NT // 2)
        dve.wait_ge(inv_out, 1)
        step(v.tensor_scalar(vm[:], ps[:, 6, 0:SLOTS], -1.0, None, ALU.add))
        step(v.tensor_scalar(inv[:], ps[:, 6, 0:SLOTS], 0.0, float(OOB), ALU.is_equal, ALU.mult))
        step(v.tensor_copy(w_inv[:], ps[:, 6, SLOTS:2 * SLOTS]))
        step(v.tensor_tensor(wgt[:], ps[:, 6, 2 * SLOTS:3 * SLOTS], w_inv[:], ALU.add))
        step(v.tensor_scalar(v_f[:], vm[:], 0.0, None, ALU.max))
        step(v.tensor_copy(v_i[:], v_f[:]))
        step(v.tensor_scalar(v_i[:], v_i[:], SEQ - 1, None, ALU.bitwise_and))
        step(v.tensor_copy(v_f[:], v_i[:]))
        step(v.tensor_tensor(gidx[:], v_f[:], inv[:], ALU.add))
        step(v.tensor_tensor(sidx[:], vm[:], inv[:], ALU.add))
        dve.wait_ge(tab_out, 1)
        v.tensor_copy(slot_tab[0:1, 0:3 * SLOTS].rearrange("p (k s) -> p k s", s=SLOTS),
                      ps[0:1, 5, 0:3 * P].rearrange("p (k s) -> p k s", s=P)[:, :, 0:SLOTS]).then_inc(tables, 1)

        def gu_low(e1, c):
            dve.wait_ge(gu_h, e1 * GUC + c + 1)
            v.tensor_tensor(gu_lo[:, c, :], stage[:, c, :], gu_hi[:, c, :].bitcast(F32), ALU.subtract).then_inc(gu_l, 1)

        def xt_low(count):
            dve.wait_ge(xt_h, count)
            for b in range(2):
                ins = v.tensor_tensor(xt_lo[:, 4 * b:4 * b + 4, :], split8(ps[:, 4 + b, :]),
                                      xt_hi[:, 4 * b:4 * b + 4, :].bitcast(F32), ALU.subtract)
            ins.then_inc(xt_l, 1)

        def ht_low(s):
            dve.wait_ge(ht_h, s + 1)
            v.tensor_tensor(ht_lo[:], split8(ps[:, 6, :]), ht_hi[:].bitcast(F32), ALU.subtract).then_inc(ht_l, 1)

        dve.wait_ge(gu_l, GUC)
        dve.wait_ge(tables, 1)
        last = dve.value_load(slot_tab[0:1, 3 * SLOTS:3 * SLOTS + 1], min_val=NE - 1, max_val=MAX_LAST)

        def body_c(s, first_step):
            g = 0 if first_step else s + 1
            e = dve.value_load(slot_tab[0:1, bass.ds(g, 1)], min_val=0, max_val=NE - 1) if not first_step else 0
            beg = dve.value_load(slot_tab[0:1, bass.ds(g + SLOTS, 1)], min_val=0, max_val=1) if not first_step else 1
            end = dve.value_load(slot_tab[0:1, bass.ds(g + 2 * SLOTS, 1)] if not first_step else
                                 slot_tab[0:1, 2 * SLOTS:2 * SLOTS + 1], min_val=0, max_val=1)
            with dve.If(end > 0):
                for c in range(GUC):
                    gu_low(e + 1, c)
                    if c == 3 and not first_step:
                        ht_low(s)
            with dve.Else():
                if not first_step:
                    ht_low(s)
                else:
                    dve.wait_ge(gu_used, 1)
            dve.wait_ge(sil_done, g + 1)
            v.tensor_tensor(hid[:], ps[:, 1, :], sil[:], ALU.mult).then_inc(hid_done, 1)
            xt_low(g + 2)

            def dn_low():
                for c in range(DNC):
                    dve.wait_ge(dn_h, e * DNC + c + 1)
                    v.tensor_tensor(dn_lo[:, c, :], stage[:, GUC + c, :], dn_hi[:, c, :].bitcast(F32),
                                    ALU.subtract).then_inc(dn_l, 1)
            if first_step:
                dn_low()
            else:
                with dve.If(beg > 0):
                    dn_low()
                dve.nop()

        xt_low(1)
        body_c(None, True)
        with dve.Fori(0, MAX_LAST) as s:
            with dve.If(s < last):
                body_c(s, False)
        ht_low(last)

        def f_out(t):
            dve.wait_ge(froot, t + 1)
            step(v.reciprocal(stat[:, 2, FC + t:FC + t + 1], stat[:, 1, FC + t:FC + t + 1]))
            v.scalar_tensor_tensor(out=ys[:, t, 1, :], in0=ys[:, t, 0, :], scalar=stat[:, 2, FC + t:FC + t + 1],
                                   in1=g_fin_b[:], op0=ALU.mult, op1=ALU.mult).then_inc(o_done, 1)

        dve.wait_ge(g3_in, 16)
        for t in range(NT):
            dve.wait_ge(ys_full[t], 32)
            step(v.tensor_tensor(split8(ys[:, t, 0, :]), rows(t), split8(ys[:, t, 0, :]), ALU.add))
            v.tensor_tensor(ys[:, t, 0, :], ys[:, t, 0, :], ys[:, t, 1, :], ALU.add).then_inc(z_done, 1)
            if t >= 1:
                dve.wait_ge(z_done, t + 1)
                f_out(t - 1)
        f_out(NT - 1)

    @block.tensor
    def _(pe):
        mm = nc.tensor.matmul

        def three(o, s_hi, s_lo, m_hi_, m_lo_, start, stop):
            mm(o, s_hi, m_hi_, start=start, stop=False)
            mm(o, s_hi, m_lo_, start=False, stop=False)
            return mm(o, s_lo, m_hi_, start=False, stop=stop)

        pe.wait_ge(consts, 2)

        def turn(src, banks, step_k):
            for k in range(KD):
                ins = nc.tensor.transpose(ps[:, banks + k // 4, (k % 4) * P:(k % 4 + 1) * P],
                                          src[:, k:D:KD] if step_k else src[:, k * P:(k + 1) * P], ident[:])
            return ins

        def a0_turn(n, half):
            pe.wait_ge(scaled, n + 1)
            if not isinstance(n, int) or n >= 2:
                pe.wait_ge(xl_done, n - 1)
            turn(x_sc[:, half, :], 2 * half, False).then_inc(turned, 1)

        a0_turn(0, 0)
        a0_turn(1, 1)
        with pe.Fori(0, 3) as i:
            for h in range(2):
                a0_turn(2 * i + 2 + h, h)
        a0_turn(8, 0)
        pe.wait_ge(xl_done, 9)

        with pe.Fori(0, NJ) as j:
            for q in range(ROLES):
                pe.wait_ge(wi_l, ROLES * j + q + 1)
                for b, (t0, n) in enumerate(BLK):
                    if q == GL:
                        pe.wait_ge(ev_dve, 9 * j + b + 1)
                    elif q == CC:
                        pe.wait_ge(ev_act, 6 * j + b + 1)
                    elif q == VV:
                        pe.wait_ge(ev_dve, 9 * j + 3 + b + 1)
                    elif q == BB:
                        pe.wait_ge(ev_act, 6 * j + 3 + b + 1)
                    for k in range(KD):
                        ins = three(ps[:, 3 * (q % 2) + b, 0:n], wi_hi[:, q, k * P:(k + 1) * P], wi_lo[:, q, k * P:(k + 1) * P],
                                    xn_hi[:, k, t0:t0 + n], xn_lo[:, k, t0:t0 + n], k == 0, k == KD - 1)
                    ins.then_inc(proj, 1)

        pe.wait_ge(ev_dve, 3 + 9 * (NJ - 1) + 6)
        for j in range(NJ):
            pe.wait_ge(conv_done, j + 1)
            for h in range(2):
                ins = mm(ps[:, 4 + h, :], ones_cw[:], mix[:, j, half(h)], start=j == 0, stop=j == NJ - 1)
                if j == NJ - 1:
                    ins.then_inc(mean_done, 1)
        for h in range(2):
            for j in range(NJ):
                pe.wait_ge(sq_done, h * NJ + j + 1)
                ins = mm(ps[:, 6 + h, :], ones_cw[:], sq[:, h, j, :], start=j == 0, stop=j == NJ - 1)
            ins.then_inc(var_done, 1)

        def out_proj(t, par):
            pe.wait_ge(ml_done, t + 1)
            if not isinstance(t, int) or t >= 2:
                pe.wait_ge(h_done, t - 1)
            for b in range(2):
                for k in range(KD):
                    ins = three(ps[:, 2 * par + b, :], m_hi[:, par, k, :], m_lo[:, par, k, :],
                                wo_hi[:, k, 512 * b:512 * b + 512], wo_lo[:, k, 512 * b:512 * b + 512], k == 0, k == KD - 1)
            ins.then_inc(op_done, 1)

        def turn_h(t, par):
            pe.wait_ge(hn_done, t + 1)
            if not isinstance(t, int) or t >= 1:
                pe.wait_ge(hnt_done, t)
            turn(hn[:, par, :], 4, False).then_inc(hturned, 1)

        def router(t, par):
            pe.wait_ge(hnt_done, t + 1)
            for k in range(KD):
                ins = mm(ps[:, 6 + par, 0:NL], hn_t[:, k, :], w_rt_sb[:, k, :], start=k == 0, stop=k == KD - 1)
            ins.then_inc(rt_done, 1)

        pe.wait_ge(wo_l, KD)
        pe.wait_ge(param_in[2], 16)
        out_proj(0, 0)
        out_proj(1, 1)
        turn_h(0, 0)
        with pe.Fori(0, 3) as i:
            for k in range(2):
                out_proj(2 * i + 2 + k, k)
                router(2 * i + k, k)
                turn_h(2 * i + 1 + k, 1 - k)
        router(6, 0)
        turn_h(7, 1)
        router(7, 1)

        pe.wait_ge(rconsts, 9)
        pe.wait_ge(a_ready, 1)
        a_all = a12[:].rearrange("p t e -> p (t e)")
        mm(ps[:, 7, 0:256], tri[:], a_all, start=True, stop=True)
        mm(ps[:, 7, 256:512], ones[:], a_all, start=True, stop=True).then_inc(ranks, 1)
        pe.wait_ge(tab_in, 1)
        for k in range(3):
            ins = mm(ps[0:1, 5, k * P:(k + 1) * P], tab[:, k:k + 1], ident[:], start=True, stop=True)
        ins.then_inc(tab_out, 1)
        pe.wait_ge(inv_in, 4)
        for a in range(2 * NT):
            ins = mm(ps[:, 6, 0:3 * SLOTS], one_r[:, a, :], val_s[:, a].rearrange("p k s -> p (k s)"),
                     start=a == 0, stop=a == 2 * NT - 1)
        ins.then_inc(inv_out, 1)

        def turn_x(count):
            pe.wait_ge(gathered, count * 16)
            turn(x_g[:], 4, True).then_inc(xt_done, 1)

        def turn_hid(s):
            pe.wait_ge(hid_done, s + 1)
            for k in range(KF):
                ins = nc.tensor.transpose(ps[:, 6, k * P:(k + 1) * P], hid[:, k:F:KF], ident[:])
            ins.then_inc(ht_done, 1)

        def gate_up(g, e, middle):
            pe.wait_ge(xt_l, g + 1)
            if middle is not None:
                pe.wait_ge(hid_done, middle + 1)
            for c in range(GUC):
                pe.wait_ge(gu_l, e * GUC + c + 1)
                for kk in range(2):
                    k = 2 * (c // 2) + kk
                    cols = slice(512 * kk, 512 * kk + 512)
                    ins = three(ps[:, c % 2, :], xt_hi[:, k, :], xt_lo[:, k, :], gu_hi[:, c, cols], gu_lo[:, c, cols],
                                k == 0, k == KD - 1)
                ins.then_inc(gu_used, 1)
                if c == 3 and middle is not None:
                    turn_hid(middle)

        def down(s, e):
            pe.wait_ge(ht_l, s + 1)
            for c in range(DNC):
                pe.wait_ge(dn_l, e * DNC + c + 1)
                for n in range(2):
                    cols = slice(512 * n, 512 * n + 512)
                    ins = three(ps[:, 2 + n, :], ht_hi[:, c, :], ht_lo[:, c, :], dn_hi[:, c, cols], dn_lo[:, c, cols],
                                c == 0, c == DNC - 1)
                ins.then_inc(dn_used, 1)

        pe.wait_ge(tables, 1)
        last = pe.value_load(slot_tab[0:1, 3 * SLOTS:3 * SLOTS + 1], min_val=NE - 1, max_val=MAX_LAST)
        turn_x(1)
        gate_up(0, 0, None)
        pe.wait_ge(xt_l, 1)
        turn_x(2)
        with pe.Fori(0, MAX_LAST) as s:
            with pe.If(s < last):
                e = pe.value_load(slot_tab[0:1, bass.ds(s + 1, 1)], min_val=0, max_val=NE - 1)
                e_before = pe.value_load(slot_tab[0:1, bass.ds(s, 1)], min_val=0, max_val=NE - 1)
                gate_up(s + 1, e, s)
                pe.wait_ge(xt_l, s + 2)
                turn_x(s + 3)
                down(s, e_before)
        turn_hid(last)
        down(last, NE - 1)

    block_cm.__exit__(None, None, None)


def kernel(x, meta_tokens, norm_mix_g, w_in, conf_dw_w, conf_dw_b, conf_ln_g, conf_ln_b, sc_conv_w, w_out, norm_ffn_g,
           w_router_group, b_router_group, w_router_expert, b_router_expert, w_exp_gate, w_exp_up, w_exp_down,
           final_norm_g):
    import numpy as np
    import concourse.bacc as bacc
    from concourse.bass_utils import run_bass_kernel_spmd

    a = {k: np.ascontiguousarray(v) for k, v in dict(
        x=x, meta=meta_tokens, w_in=w_in, w_out=w_out, g_mix=norm_mix_g, g_ffn=norm_ffn_g, g_fin=final_norm_g,
        cw=conf_dw_w, cb=conf_dw_b, lg=conf_ln_g, lb=conf_ln_b, sw=sc_conv_w, rg=w_router_group, bg=b_router_group,
        re=w_router_expert, be=b_router_expert, wg=w_exp_gate, wu=w_exp_up, wd=w_exp_down).items()}
    parts = a["w_in"][0].reshape(KD, P, 5, NJ, P)[:, :, [1, 0, 3, 4, 2]]
    w_in_l = np.ascontiguousarray(parts.transpose(3, 2, 1, 0, 4)).reshape(NJ * ROLES, P, KD * P)
    chan = np.concatenate([a["cw"][0], a["cb"], a["lg"], a["lb"], a["sw"][0]], axis=0)
    chan = np.ascontiguousarray(chan.reshape(NCH, NJ, P).transpose(2, 1, 0)).reshape(P, NJ * NCH)
    arrays = {
        "x": a["x"][0], "meta": a["meta"], "w_in": w_in_l, "chan": chan, "g_mix": a["g_mix"][0], "w_out": a["w_out"][0],
        "g_ffn": a["g_ffn"][0],
        "w_rt": np.ascontiguousarray(np.concatenate([a["rg"][0], a["re"][0]], axis=1)),
        "b_rt": np.ascontiguousarray(np.concatenate([a["bg"][0], a["be"][0]])),
        "w_gate": a["wg"][0], "w_up": a["wu"][0], "w_down": a["wd"][0], "g_fin": a["g_fin"],
    }
    nc = bacc.Bacc("TRN2", target_bir_lowering=False, num_devices=1)
    args = [nc.dram_tensor(f"in_{k}", v.shape, mybir.dt.from_np(v.dtype), kind="ExternalInput").ap()
            for k, v in arrays.items()]
    args.append(nc.dram_tensor("out_0", (SEQ, D), F32, kind="ExternalOutput").ap())
    trunk(nc, *args)
    r = run_bass_kernel_spmd(nc, [{f"in_{k}": v for k, v in arrays.items()}], core_ids=[0])
    return r.results[0]["out_0"].reshape(1, SEQ, D)
```

```python
import concourse.bass as bass
from concourse import mybir
from concourse.alu_op_type import AluOpType as ALU

ACT = mybir.ActivationFunctionType
AX = mybir.AxisListType
F32 = mybir.dt.float32
F32R = mybir.dt.float32r
I32 = mybir.dt.int32
U32 = mybir.dt.uint32

P = 128
D = 1024
KD = D // P
META = 16
SEQ = 1024
NT = SEQ // P
TG = META + SEQ
CW = 512
NJ = CW // P
TAPS, STAPS = 31, 3
HELP = 12
PAD = TAPS - 1 - META
ROLES = 5
GL, UU, CC, VV, BB = range(ROLES)
NX = 4
BLK = [(0, 348), (348, 346), (694, 346)]
NCH = TAPS + 3 + STAPS
CB, LG, LB, SW = TAPS, TAPS + 1, TAPS + 2, TAPS + 3
NG, NEG = 4, 8
NE = NG * NEG
NL = NG + NE
F = 512
KF = F // P
GUC, DNC = 8, 4
NC = GUC + DNC
AHEAD = DNC
RING = 6
MAXB = 2 * SEQ // P
MAX_LAST = NE + MAXB - 2
SLOTS = MAX_LAST + 4
EPS = 1e-6
HALF = P // 2
OOB = 4096


class Tally:

    def __init__(self, eng, sem):
        self.eng, self.sem, self.n, self.term = eng, sem, 0, None

    def value(self):
        return self.n if self.term is None else self.term + self.n

    def step(self, ins):
        ins.then_inc(self.sem, 1)
        self.n += 1
        self.eng.wait_ge(self.sem, self.value())

    def loop(self, i, per):
        self.saved, self.per = self.n, per
        self.term = i * per

    def end(self, trips):
        assert self.n - self.saved == self.per, (self.n - self.saved, self.per)
        self.n = self.saved + self.per * trips
        self.term = None


def trunk(nc, x, meta, w_in, chan, g_mix, w_out, g_ffn, w_rt, b_rt, w_gate, w_up, w_down, g_fin, out):
    hn_rows = nc.dram_tensor("hn_rows", (SEQ, D), F32).ap()
    y_rows = nc.dram_tensor("y_rows", (2 * SEQ, D), F32).ap()

    R1, R2, R3, R4, ST, SM = 0, 66560, 107520, 140288, 157056, 206208
    base0 = (nc.sbuf_base + 31) // 32 * 32

    def at(name, shape, dt, offset):
        return nc.alloc_sbuf_tensor_at(name, shape, dt, offset=base0 + offset)

    class Bump:
        def __init__(self, start, end):
            self.o, self.end = start, end

        def __call__(self, name, shape, dt=F32):
            n = 4
            for s in shape[1:]:
                n *= s
            t = at(name, shape, dt, self.o)
            self.o += (n + 31) // 32 * 32
            assert self.o <= self.end, (name, self.o, self.end)
            return t

    xn_hi = at("xn_hi", [P, KD, TG], F32R, R1)
    xn_lo = at("xn_lo", [P, KD, TG], F32R, R1 + KD * TG * 4)
    wi_hi = at("wi_hi", [P, ROLES, KD * P], F32R, R2)
    wi_lo = at("wi_lo", [P, ROLES, KD * P], F32R, R2 + ROLES * KD * P * 4)
    mix = at("mix", [P, KD, SEQ], F32, R3)
    r = Bump(R3, R4)
    x_in = r("x_in", [P, NX, D])
    x_sc = r("x_sc", [P, 2, D])
    g_mix_b = r("g_mix_b", [P, D])
    x_sq = r("x_sq", [P, D])
    r = Bump(R4, ST)
    a_buf = r("a_buf", [P, PAD + TG])
    cv = r("cv", [P, TG])
    sig = r("sig", [P, TG])
    c_sb = r("c_sb", [P, TG])
    r = Bump(R4, ST)
    sq = r("sq", [P, 2, NJ, 512])
    wo_hi = at("wo_hi", [P, KD, D], F32R, R1)
    wo_lo = at("wo_lo", [P, KD, D], F32R, R1 + KD * D * 4)
    r = Bump(R2, R3)
    m_hi = r("m_hi", [P, 2, KD, P], F32R)
    m_lo = r("m_lo", [P, 2, KD, P], F32R)
    x_res = r("x_res", [P, 2, D])
    std = at("std", [P, 2, 512], F32, r.o)
    rstd = at("rstd", [P, 2, 512], F32, r.o + 4096)
    hn = r("hn", [P, 2, D])
    hn_t = r("hn_t", [P, KD, P])
    g_ffn_b = r("g_ffn_b", [P, D])
    r = Bump(R4, ST)
    tri = r("tri", [P, P])
    ones = r("ones", [P, P])
    tri_r = r("tri_r", [P, P], F32R)
    ones_r = r("ones_r", [P, P], F32R)
    iota_r = r("iota_r", [P, P])
    iota_s = r("iota_s", [P, SLOTS])
    part = r("part", [P, 1])
    rev = r("rev", [P, NEG])
    thr = r("thr", [P, 7, NE])
    asg_id = r("asg_id", [P, 2, NT])
    a1 = r("a1", [P, NT, NG, NEG])
    a2 = r("a2", [P, NT, NG, NEG])
    a12 = r("a12", [P, NT, NE], F32R)
    dest = r("dest", [P, NT, NE])
    prod = r("prod", [P, NT, NE])
    more = r("more", [P, 7, NE])
    b_sq = r("b_sq", [P, D])
    r = Bump(R2, R3)
    one_r = r("one_r", [P, 2 * NT, P], F32R)
    one_s = r("one_s", [P, 2 * NT, SLOTS])
    val_s = r("val_s", [P, 2 * NT, 3, SLOTS], F32R)
    g_sh = r("g_sh", [P, NT, NG])
    g_ex = r("g_ex", [P, NT, NG])
    g_one = r("g_one", [P, NT, NG])
    g_key = r("g_key", [P, NT, NG])
    sel = r("sel", [P, NT, NEG])
    sel2 = r("sel2", [P, NT, NEG])
    key = r("key", [P, NT, NEG])
    o1 = r("o1", [P, NT, NEG])
    o2 = r("o2", [P, NT, NEG])
    vec = r("vec", [P, 12, NT])
    wk = r("wk", [P, 2, NT])
    wk_hi = r("wk_hi", [P, 2, NT], F32R)
    wk_lo = r("wk_lo", [P, 2, NT], F32R)
    w_inv = r("w_inv", [P, SLOTS])
    id_inv = r("id_inv", [P, SLOTS])
    dd = r("dd", [P, 2, NT])
    dd_i = r("dd_i", [P, 2, NT], I32)
    sl_i = r("sl_i", [P, 2, NT], I32)
    ro_i = r("ro_i", [P, 2, NT], I32)
    sl_f = r("sl_f", [P, 2, NT])
    ro_f = r("ro_f", [P, 2, NT])
    count = r("count", [P, NE])
    nblk = r("nblk", [P, NE])
    s_end = r("s_end", [P, NE])
    s_beg = r("s_beg", [P, NE])
    junk = r("junk", [P, NE])
    tab = r("tab", [P, 1])
    raw = at("raw", [P, ST // 4 + NC * D], F32, R1)
    ring = [at(f"ring{i}", [P, 2, D], F32R, R1 + NC * D * 4 + 8 * D * i if i < 2 else R2 + 8 * D * (i - 2))
            for i in range(RING)]
    xt_hi = at("xt_hi", [P, KD, P], F32R, R2 + 8 * D * (RING - 2))
    xt_lo = at("xt_lo", [P, KD, P], F32R, R2 + 8 * D * (RING - 2) + D * 4)
    r = Bump(R4, ST)
    ht_hi = r("ht_hi", [P, KF, P], F32R)
    ht_lo = r("ht_lo", [P, KF, P], F32R)
    x_g = r("x_g", [P, D])
    y_sb = r("y_sb", [P, D])
    hid = r("hid", [P, F])
    sil = r("sil", [P, F])
    r = Bump(R1, R3)
    ys = r("ys", [P, NT, 2, D])
    f_sq = r("f_sq", [P, D])
    g_fin_b = at("g_fin_b", [P, D], F32, R2 + 8 * D * (RING - 2))

    stage = at("stage", [P, NC, D], F32, ST)
    tap_mul = [at(f"tap_mul{i}", [P, SEQ], F32, ST + (1 + i) * D * 4) for i in range(2)]
    tap_sum = at("tap_sum", [P, SEQ], F32, ST + 3 * D * 4)
    r = Bump(SM, SM + 6624)
    ident = r("ident", [P, P])
    ones_cw = r("ones_cw", [P, P])
    chan_sb = r("chan_sb", [P, NJ * NCH])
    logit = r("logit", [P, NT, NL])
    w_rt_sb = r("w_rt_sb", [P, KD, NL])
    b_rt_b = r("b_rt_b", [P, NL])
    stat = r("stat", [P, 3, 32])
    eps = r("eps", [P, 1])
    unread = r("unread", [P, 1])
    gidx = r("gidx", [P, SLOTS], I32)
    sidx = r("sidx", [P, SLOTS], I32)
    wgt = r("wgt", [P, SLOTS])
    gidx_cur = r("gidx_cur", [P, 1], I32)
    sidx_cur = r("sidx_cur", [P, 1], I32)
    slot_expert = r("slot_expert", [1, SLOTS], I32)
    slot_even = r("slot_even", [1, SLOTS], I32)
    slot_big = r("slot_big", [1, SLOTS], I32)
    expert_last = r("expert_last", [1, NE], I32)

    ps = nc.alloc_psum_tensor("ps", [P, 8, 512], F32)

    def sem(name):
        return nc.alloc_semaphore(name)

    param_in = [sem(f"param_in{i}") for i in range(5)]
    g2_in = sem("g2_in")
    g3_in = sem("g3_in")
    x_full = [sem(f"x_full{i}") for i in range(NX)]
    wi_full = [sem(f"wi_full{i}") for i in range(ROLES)]
    wo_full = [sem(f"wo_full{i}") for i in range(KD)]
    xr_full = [sem(f"xr_full{i}") for i in range(2)]
    hn_out = [sem(f"hn_out{i}") for i in range(2)]
    st_full = [sem(f"st_full{i}") for i in range(NC)]
    consts = sem("consts")
    rconsts = sem("rconsts")
    pool_own = sem("pool_own")
    act_own = sem("act_own")
    dve_own = sem("dve_own")
    eps_ok = sem("eps_ok")
    meta_zero = sem("meta_zero")
    root = sem("root")
    scaled = sem("scaled")
    turned = sem("turned")
    xh_done = sem("xh_done")
    xl_done = sem("xl_done")
    wi_h = sem("wi_h")
    wi_l = sem("wi_l")
    proj = sem("proj")
    ev_act = sem("ev_act")
    ev_dve = sem("ev_dve")
    tap_ready = sem("tap_ready")
    tap_added = sem("tap_added")
    conv_done = sem("conv_done")
    mean_done = sem("mean_done")
    cent_done = sem("cent_done")
    sq_done = sem("sq_done")
    var_done = sem("var_done")
    std_done = sem("std_done")
    nrm_done = sem("nrm_done")
    silu_done = sem("silu_done")
    wo_h = sem("wo_h")
    wo_l = sem("wo_l")
    mh_done = sem("mh_done")
    ml_done = sem("ml_done")
    op_done = sem("op_done")
    h_done = sem("h_done")
    hroot = sem("hroot")
    hn_done = sem("hn_done")
    hturned = sem("hturned")
    hnt_done = sem("hnt_done")
    rt_done = sem("rt_done")
    lg_done = sem("lg_done")
    exp_in = sem("exp_in")
    exp_out = sem("exp_out")
    a_ready = sem("a_ready")
    ranks = sem("ranks")
    inv_in = sem("inv_in")
    inv_out = sem("inv_out")
    tab_in = sem("tab_in")
    tab_out = sem("tab_out")
    tables = sem("tables")
    part_h = sem("part_h")
    part_l = sem("part_l")
    used = sem("used")
    gidx_ready = sem("gidx_ready")
    idx_ok = sem("idx_ok")
    xg_zero = sem("xg_zero")
    gathered = sem("gathered")
    xt_done = sem("xt_done")
    xt_h = sem("xt_h")
    xt_l = sem("xt_l")
    sil_done = sem("sil_done")
    hid_done = sem("hid_done")
    ht_done = sem("ht_done")
    ht_h = sem("ht_h")
    ht_l = sem("ht_l")
    y_ev = sem("y_ev")
    y_out = sem("y_out")
    ys_full = [sem(f"ys_full{i}") for i in range(NT)]
    z_done = sem("z_done")
    froot = sem("froot")
    o_done = sem("o_done")
    o_out = [sem(f"o_out{i}") for i in range(2)]

    EV_A, EV_D = 6, 9
    WO_SLOT = [5, 6, 7, 8, 9, 10, 11, 0]
    A0C, BC, FC = 0, 9, 17

    def bank(q, b):
        return ps[:, (3 * q + b) % 8, :]

    def tile_cols(n):
        return (0, META) if n == 0 else (META + (n - 1) * P, P)

    def rows(t):
        return mix[:, :, bass.ds(t * P, P)] if not isinstance(t, int) else mix[:, :, t * P:(t + 1) * P]

    def raw_chunk(even, c):
        if isinstance(even, int):
            o = even * (ST // 4) + c * D
            return raw[:, o:o + D]
        return raw[:, bass.ds(even * (ST // 4) + c * D, D)]

    def half(h):
        return slice(512 * h, 512 * h + 512)

    def quarter(q):
        return slice(256 * q, 256 * q + 256)

    def split8(ap):
        return ap.rearrange("p (k c) -> p k c", c=P)

    block_cm = nc.Block()
    block = block_cm.__enter__()

    @block.sync
    def _(sp):
        sp.wait_ge(meta_zero, 1)
        sp.dma_start(x_in[0:META, 0, :], meta).then_inc(x_full[0], 16)
        sp.dma_start(g_mix_b[:], g_mix.partition_broadcast(P)).then_inc(param_in[0], 16)
        for n in range(1, NX):
            sp.dma_start(x_in[:, n, :], x[(n - 1) * P:n * P, :]).then_inc(x_full[n], 16)
        sp.dma_start(stage[:, GL, :], w_in[GL]).then_inc(wi_full[GL], 16)
        for n in range(NX, NT + 1):
            if n == NT:
                sp.dma_start(stage[:, UU, :], w_in[UU]).then_inc(wi_full[UU], 16)
            sp.wait_ge(scaled, n - NX + 1)
            sp.dma_start(x_in[:, n % NX, :], x[(n - 1) * P:n * P, :]).then_inc(x_full[n % NX], 16)
        sp.dma_start(chan_sb[:], chan).then_inc(param_in[1], 16)
        for q in (CC, VV, BB):
            sp.dma_start(stage[:, q, :], w_in[q]).then_inc(wi_full[q], 16)
        for k in range(KD - 1):
            sp.dma_start(stage[:, WO_SLOT[k], :], w_out[k * P:(k + 1) * P, :]).then_inc(wo_full[k], 16)
        sp.dma_start(w_rt_sb[:], w_rt.rearrange("(k p) n -> p k n", p=P)).then_inc(param_in[2], 16)
        sp.dma_start(b_rt_b[:], b_rt.partition_broadcast(P)).then_inc(param_in[3], 16)
        with sp.Fori(0, NJ - 1) as j:
            for q in range(ROLES):
                sp.wait_ge(wi_l, ROLES * j + q + 1)
                sp.dma_start(stage[:, q, :], w_in[bass.ds(ROLES * j + ROLES + q, 1)]
                             .rearrange("a p n -> (a p) n")).then_inc(wi_full[q], 16)
        sp.wait_ge(wi_l, ROLES * NJ)
        sp.dma_start(stage[:, WO_SLOT[7], :], w_out[7 * P:8 * P, :]).then_inc(wo_full[7], 16)
        sp.wait_ge(proj, NJ * ROLES * 3)
        sp.dma_start(g_ffn_b[:], g_ffn.partition_broadcast(P)).then_inc(g2_in, 16)
        for t in range(2):
            sp.dma_start(x_res[:, t, :], x[t * P:(t + 1) * P, :]).then_inc(xr_full[t], 16)

        def load_chunk(e, c, even):
            if c < GUC:
                src, k, q = (w_up if c % 2 else w_gate), KD, c // 2
            else:
                src, k, q = w_down, KF, c - GUC
            if isinstance(e, int):
                ap = src[e].rearrange("(p k) f -> p (k f)", k=k)
            else:
                ap = src[bass.ds(e, 1)].rearrange("a (p k) f -> (a p) (k f)", k=k)
            if not isinstance(e, int) or e:
                sp.wait_ge(st_full[c], e * 16)
            sp.dma_start(raw_chunk(even, c), ap[:, q * D:(q + 1) * D]).then_inc(st_full[c], 16)

        sp.wait_ge(wo_l, KD)
        sp.wait_ge(conv_done, NJ)
        for c in range(NC):
            load_chunk(0, c, 1)
        with sp.Fori(0, 3) as i:
            for par in range(2):
                sp.wait_ge(hn_done, 2 * i + par + 1)
                sp.dma_start(hn_rows[bass.ds((2 * i + par) * P, P), :], hn[:, par, :]).then_inc(hn_out[par], 16)
                sp.dma_start(x_res[:, par, :], x[bass.ds((2 * i + par + 2) * P, P), :]).then_inc(xr_full[par], 16)
        for t in (6, 7):
            sp.wait_ge(hn_done, t + 1)
            sp.dma_start(hn_rows[t * P:(t + 1) * P, :], hn[:, t % 2, :]).then_inc(hn_out[t % 2], 16)
        sp.wait_ge(op_done, NT)
        for c in range(NC):
            load_chunk(1, c, 0)
        sp.wait_ge(tables, 1)

        def last_slot(e):
            return sp.value_load(expert_last[0:1, bass.ds(e, 1)] if not isinstance(e, int) else expert_last[0:1, e:e + 1],
                                 min_val=0, max_val=MAX_LAST)

        def load_gate_up(e, even):
            slot = last_slot(e - 2)
            for c in range(GUC):
                sp.wait_ge(part_l, slot * NC + c + 1)
                load_chunk(e, c, even)

        def load_down(e, even):
            slot = last_slot(e - 2)
            for c in range(GUC, NC):
                sp.wait_ge(part_l, slot * NC + NC + c + 1)
                load_chunk(e, c, even)

        load_gate_up(2, 1)
        with sp.Fori(0, (NE - 4) // 2) as i:
            load_gate_up(2 * i + 3, 0)
            load_down(2 * i + 2, 1)
            load_gate_up(2 * i + 4, 1)
            load_down(2 * i + 3, 0)
        load_gate_up(NE - 1, 0)
        load_down(NE - 2, 1)
        load_down(NE - 1, 0)
        last = sp.value_load(expert_last[0:1, NE - 1:NE], min_val=NE - 1, max_val=MAX_LAST)
        sp.wait_ge(xt_l, last + 2)
        sp.wait_ge(used, last * NC + GUC - DNC)
        sp.dma_start(g_fin_b[:], g_fin.partition_broadcast(P)).then_inc(g3_in, 16)
        sp.wait_ge(y_out, last * 16 + 16)
        for t in range(NT):
            for k in range(2):
                sp.dma_start(ys[:, t, k, :], y_rows[k * SEQ + t * P:k * SEQ + (t + 1) * P, :]).then_inc(ys_full[t], 16)
        for t in range(NT):
            sp.wait_ge(o_done, t + 1)
            sp.dma_start(out[t * P:(t + 1) * P, :], ys[:, t, 1, :]).then_inc(o_out[t % 2], 16)
        for h in range(2):
            sp.wait_ge(o_out[h], 16 * NT // 2)

    @block.gpsimd
    def _(pool):
        own = Tally(pool, pool_own)
        nc.gpsimd.memset(x_in[:, 0, :], 0.0).then_inc(meta_zero, 1)
        own.step(nc.gpsimd.memset(ident[:], 0.0))
        nc.gpsimd.affine_select(out=ident[:], in_=ident[:], compare_op=ALU.not_equal, fill=1.0, base=0,
                                pattern=[[-1, P]], channel_multiplier=1).then_inc(consts, 1)
        nc.gpsimd.memset(ones_cw[:], 1.0 / CW).then_inc(consts, 1)

        def wi_low(q, count):
            pool.wait_ge(wi_h, count)
            nc.gpsimd.tensor_tensor(wi_lo[:, q, :], stage[:, q, :], wi_hi[:, q, :].bitcast(F32),
                                    ALU.subtract).then_inc(wi_l, 1)

        with pool.Fori(0, NJ) as j:
            for q in range(ROLES):
                wi_low(q, ROLES * j + q + 1)
        for i in range(1, HELP):
            pool.wait_ge(tap_ready, i + 1)
            if i > 1:
                pool.wait_ge(tap_added, i - 1)
            nc.gpsimd.tensor_tensor(tap_sum[:], tap_sum[:], tap_mul[i % 2][:], ALU.add).then_inc(tap_added, 1)
        for k in range(KD):
            pool.wait_ge(wo_h, k + 1)
            nc.gpsimd.tensor_tensor(wo_lo[:, k, :], stage[:, WO_SLOT[k], :], wo_hi[:, k, :].bitcast(F32),
                                    ALU.subtract).then_inc(wo_l, 1)
        pool.wait_ge(var_done, 2)
        own.step(nc.gpsimd.memset(ones[:], 1.0))
        own.step(nc.gpsimd.memset(tri[:], 1.0))
        own.step(nc.gpsimd.affine_select(out=tri[:], in_=tri[:], compare_op=ALU.is_gt, fill=0.0, base=0,
                                         pattern=[[1, P]], channel_multiplier=-1))
        nc.gpsimd.tensor_copy(ones_r[:], ones[:]).then_inc(rconsts, 1)
        nc.gpsimd.tensor_copy(tri_r[:], tri[:]).then_inc(rconsts, 1)
        for ap, pattern, base, cm in (
                (iota_r[:], [[1, P]], 0, 0), (iota_s[:], [[1, SLOTS]], 0, 0), (part[:], [[0, 1]], 0, 1),
                (rev[:], [[-1, NEG]], NEG, 0), (thr[:], [[P, 7], [0, NE]], P, 0),
                (asg_id[:], [[SEQ, 2], [P, NT]], -OOB, 1)):
            nc.gpsimd.iota(ap, pattern=pattern, base=base, channel_multiplier=cm,
                           allow_small_or_imprecise_dtypes=True).then_inc(rconsts, 1)

        for h in range(2):
            pool.wait_ge(hn_out[h], 16 * NT // 2)
        pool.wait_ge(inv_in, 10)
        nc.gpsimd.memset(x_g[:], 0.0).then_inc(xg_zero, 1)
        pool.wait_ge(xg_zero, 1)
        pool.wait_ge(gidx_ready, 1)

        def column(table, g):
            return table[:, g:g + 1] if isinstance(g, int) else table[:, bass.ds(g, 1)]

        def sized(g, transfer):
            big = pool.value_load(slot_big[0:1, bass.ds(g, 1)], min_val=0, max_val=1)
            with pool.If(big > 0):
                transfer(P)
            with pool.Else():
                transfer(HALF)

        def whole(g, transfer):
            transfer(P)

        def gather(g, copies, transfer_by=sized):
            def transfer(n):
                pool.wait_ge(idx_ok, copies)
                nc.gpsimd.indirect_dma_start(
                    out=x_g[0:n, :], out_offset=None, in_=hn_rows,
                    in_offset=bass.IndirectOffsetOnAxis(ap=gidx_cur[0:n, 0:1].bitcast(U32), axis=0),
                    bounds_check=g + SEQ - 1, oob_is_err=False).then_inc(gathered, 16)

            if not isinstance(g, int) or g:
                pool.wait_ge(xt_done, g)
            nc.gpsimd.tensor_copy(gidx_cur[:], column(gidx, g)).then_inc(idx_ok, 1)
            transfer_by(g, transfer)

        def scatter(g, copies, transfer_by=sized):
            def transfer(n):
                pool.wait_ge(idx_ok, copies)
                pool.wait_ge(y_ev, g + 1)
                nc.gpsimd.indirect_dma_start(
                    out=y_rows, out_offset=bass.IndirectOffsetOnAxis(ap=sidx_cur[0:n, 0:1].bitcast(U32), axis=0),
                    in_=y_sb[0:n, :], in_offset=None,
                    bounds_check=g + 2 * SEQ - 1, oob_is_err=False).then_inc(y_out, 16)

            if not isinstance(g, int) or g:
                pool.wait_ge(y_out, g * 16)
            nc.gpsimd.tensor_copy(sidx_cur[:], column(sidx, g)).then_inc(idx_ok, 1)
            transfer_by(g, transfer)

        for g in range(3):
            gather(g, g + 1, whole)
        pool.wait_ge(tables, 1)
        last = pool.value_load(expert_last[0:1, NE - 1:NE], min_val=NE - 1, max_val=MAX_LAST)
        gather(3, 4, whole)
        scatter(0, 5, whole)
        with pool.Fori(1, MAX_LAST + 1) as i:
            with pool.If(i < last):
                gather(i + 3, 2 * i + 4)
                scatter(i, 2 * i + 5)
            with pool.Else():
                with pool.If(i < last + 1):
                    scatter(i, 2 * i + 4, whole)

    @block.scalar
    def _(act):
        own = Tally(act, act_own)
        act.wait_ge(eps_ok, 1)

        def load_table(function):
            own.step(nc.scalar.activation(unread[:], eps[:], function))

        load_table(ACT.Sqrt)

        def mean_root(src, junk_out, column, done):
            ssq = stat[:, 0, bass.ds(column, 1)] if not isinstance(column, int) else stat[:, 0, column:column + 1]
            rt = stat[:, 1, bass.ds(column, 1)] if not isinstance(column, int) else stat[:, 1, column:column + 1]
            own.step(nc.scalar.activation(junk_out, src, ACT.Square, accum_out=ssq))
            nc.scalar.activation(rt, ssq, ACT.Sqrt, bias=eps[:], scale=1.0 / D).then_inc(done, 1)

        def a0_root(n):
            act.wait_ge(x_full[n % NX], 16 * (n // NX + 1))
            mean_root(x_in[:, n % NX, :], x_sq[:], n, root)

        def a0_hi(n):
            t0, w = tile_cols(n)
            act.wait_ge(turned, n + 1)
            for b in range(2):
                ins = nc.scalar.copy(xn_hi[:, 4 * b:4 * b + 4, t0:t0 + w], split8(ps[:, 4 + 2 * (n % 2) + b, :])[:, :, 0:w])
            ins.then_inc(xh_done, 1)

        def wi_split(q, full):
            act.wait_ge(wi_full[q], full)
            nc.scalar.copy(wi_hi[:, q, :], stage[:, q, :]).then_inc(wi_h, 1)

        a0_root(0)
        for n in range(1, NT + 1):
            a0_root(n)
            a0_hi(n - 1)
            if n == 3:
                wi_split(GL, 16)
        wi_split(UU, 16)
        a0_hi(NT)
        for q in (CC, VV, BB):
            wi_split(q, 16)

        def helpers(first, end):
            for i in range(first, end):
                k = TAPS - HELP + i
                if i >= 3:
                    act.wait_ge(tap_added, i - 2)
                nc.scalar.activation(tap_mul[i % 2][:] if i else tap_sum[:], a_buf[:, k:k + SEQ], ACT.Copy,
                                     scale=chan_sb[:, (NJ - 1) * NCH + k:(NJ - 1) * NCH + k + 1]).then_inc(tap_ready, 1)

        def body_a(j, split_next):
            for b, (t0, n) in enumerate(BLK):
                act.wait_ge(proj, 15 * j + b + 1)
                nc.scalar.activation(sig[:, t0:t0 + n], bank(GL, b)[:, 0:n], ACT.Sigmoid).then_inc(ev_act, 1)
            if not split_next:
                act.wait_ge(ev_dve, EV_D * NJ + 3)
                act.wait_ge(wi_l, ROLES * NJ - 1)
                helpers(0, 5)
            else:
                wi_split(GL, 16 * j + 32)
                act.wait_ge(proj, 15 * j + 6)
                wi_split(UU, 16 * j + 32)
            for b, (t0, n) in enumerate(BLK):
                act.wait_ge(proj, 15 * j + 6 + b + 1)
                nc.scalar.copy(c_sb[:, t0:t0 + n], bank(CC, b)[:, 0:n]).then_inc(ev_act, 1)
            if not split_next:
                helpers(5, HELP)
            else:
                wi_split(CC, 16 * j + 32)
                act.wait_ge(proj, 15 * j + 12)
                wi_split(VV, 16 * j + 32)
                act.wait_ge(proj, 15 * j + 15)
                wi_split(BB, 16 * j + 32)

        with act.Fori(0, NJ - 1) as j:
            body_a(j, True)
        body_a(NJ - 1, False)

        def wo_split(first, end):
            for k in range(first, end):
                act.wait_ge(wo_full[k], 16)
                nc.scalar.copy(wo_hi[:, k, :], stage[:, WO_SLOT[k], :]).then_inc(wo_h, 1)

        act.wait_ge(proj, NJ * 15)
        wo_split(0, 5)

        def m_split(t, par):
            if not isinstance(t, int) or t >= 2:
                act.wait_ge(op_done, t - 1)
            nc.scalar.copy(m_hi[:, par], rows(t)).then_inc(mh_done, 1)

        def squares(h):
            for j in range(NJ):
                act.wait_ge(cent_done, h * NJ + j + 1)
                nc.scalar.activation(sq[:, h, j, :], mix[:, j, half(h)], ACT.Square).then_inc(sq_done, 1)

        def deviation(h):
            act.wait_ge(var_done, h + 1)
            nc.scalar.activation(std[:, h, :], ps[:, 6 + h, :], ACT.Sqrt, bias=eps[:]).then_inc(std_done, 1)

        def ln_silu(q):
            act.wait_ge(nrm_done, q + 1)
            for j in range(NJ):
                c = j * NCH
                ins = nc.scalar.activation(mix[:, j, quarter(q)], mix[:, j, quarter(q)], ACT.Silu,
                                           bias=chan_sb[:, c + LB:c + LB + 1], scale=chan_sb[:, c + LG:c + LG + 1])
            ins.then_inc(silu_done, 1)
            act.wait_ge(silu_done, q + 1)

        load_table(ACT.Sqrt)
        squares(0)
        wo_split(5, 6)
        squares(1)
        deviation(0)
        wo_split(6, KD)
        deviation(1)
        ln_silu(0)
        act.wait_ge(ev_dve, EV_D * (NJ + 1))

        m_split(0, 0)
        m_split(1, 1)
        for q in (1, 2, 3):
            ln_silu(q)

        def b_root(t):
            act.wait_ge(h_done, t + 1)
            mean_root(rows(t), split8(b_sq[:]), t + BC, hroot)

        def hnt_copy(t):
            act.wait_ge(hturned, t + 1)
            for b in range(2):
                ins = nc.scalar.copy(hn_t[:, 4 * b:4 * b + 4, :], split8(ps[:, 4 + b, :]))
            ins.then_inc(hnt_done, 1)

        b_root(0)
        with act.Fori(0, 3) as i:
            own.loop(i, 2)
            for k in range(2):
                m_split(2 * i + 2 + k, k)
                hnt_copy(2 * i + k)
                b_root(2 * i + 1 + k)
            own.end(3)
        hnt_copy(6)
        b_root(7)
        hnt_copy(7)

        act.wait_ge(exp_in, 1)
        nc.scalar.activation(g_ex[:], g_sh[:], ACT.Exp).then_inc(exp_out, 1)
        act.wait_ge(exp_in, 2)
        nc.scalar.activation(vec[:, 5, :], vec[:, 4, :], ACT.Exp).then_inc(exp_out, 1)

        def split(n, place, c, e, even):
            if not isinstance(n, int) or n >= RING:
                act.wait_ge(used, n - RING + 1)
            act.wait_ge(st_full[c], e * 16 + 16)
            nc.scalar.copy(ring[place % RING][:, 0, :], raw_chunk(even, c)).then_inc(part_h, 1)

        def xt_copy(count):
            act.wait_ge(xt_done, count)
            for b in range(2):
                ins = nc.scalar.copy(xt_hi[:, 4 * b:4 * b + 4, :], split8(ps[:, 4 + b, :]))
            ins.then_inc(xt_h, 1)

        def ht_copy(s):
            act.wait_ge(ht_done, s + 1)
            nc.scalar.copy(ht_hi[:], split8(ps[:, 6, :])).then_inc(ht_h, 1)

        def y_copy(s, count, copies):
            act.wait_ge(used, count)
            act.wait_ge(idx_ok, copies)
            for n in range(2):
                ins = nc.scalar.activation(y_sb[:, 512 * n:512 * n + 512], ps[:, 2 + n, :], ACT.Copy,
                                           scale=wgt[:, bass.ds(s, 1)])
            ins.then_inc(y_ev, 1)

        act.wait_ge(op_done, NT)
        split(0, 0, 0, 0, 1)
        split(1, 1, 1, 0, 1)
        act.wait_ge(tables, 1)
        last = act.value_load(expert_last[0:1, NE - 1:NE], min_val=NE - 1, max_val=MAX_LAST)

        def expert_of(g):
            e, even = (t[0:1, g:g + 1] if isinstance(g, int) else t[0:1, bass.ds(g, 1)]
                       for t in (slot_expert, slot_even))
            return act.value_load(e, min_val=0, max_val=NE - 1), act.value_load(even, min_val=0, max_val=1)

        xt_copy(1)
        for c in range(2, GUC):
            split(c, c, c, 0, 1)
        act.wait_ge(used, GUC)
        nc.scalar.activation(sil[:], ps[:, 0, :], ACT.Silu).then_inc(sil_done, 1)
        xt_copy(2)
        after = expert_of(1)
        for c in range(AHEAD):
            split(GUC + c, 2 + c, c, *after)
        with act.Fori(0, MAX_LAST + 1) as s:
            with act.If(s < last):
                now = expert_of(s + 1)
                n = s * NC + GUC
                for c in range(AHEAD, GUC):
                    if c == 6:
                        ht_copy(s)
                    split(n + c, 2 + c, c, *now)
                before = expert_of(s)
                for c in range(GUC, NC):
                    split(n + c, 2 + c, c, *before)
                act.wait_ge(used, n + GUC)
                nc.scalar.activation(sil[:], ps[:, 0, :], ACT.Silu).then_inc(sil_done, 1)
                xt_copy(s + 3)
                with act.If(s + 1 < last):
                    after = expert_of(s + 2)
                    for c in range(AHEAD):
                        split(n + NC + c, 2 + c, c, *after)
                with act.Else():
                    for c in range(AHEAD):
                        split(n + NC + c, 2 + c, GUC + c, *now)
                y_copy(s, n + NC, 2 * s + 5)
            with act.Else():
                with act.If(s < last + 1):
                    ht_copy(s)
                    y_copy(s, s * NC + NC, 2 * s + 4)

        load_table(ACT.Sqrt)
        for t in range(NT):
            act.wait_ge(z_done, t + 1)
            own.step(nc.scalar.activation(f_sq[:], ys[:, t, 0, :], ACT.Square, accum_out=stat[:, 0, FC + t:FC + t + 1]))
            nc.scalar.activation(stat[:, 1, FC + t:FC + t + 1], stat[:, 0, FC + t:FC + t + 1], ACT.Sqrt, bias=eps[:],
                                 scale=1.0 / D).then_inc(froot, 1)

    @block.vector
    def _(dve):
        own = Tally(dve, dve_own)
        v = nc.vector
        v.memset(eps[:], EPS).then_inc(eps_ok, 1)
        v.memset(a_buf[:, 0:PAD - 1], 0.0).then_inc(ev_dve, EV_D)
        v.memset(a_buf[:, PAD - 1:PAD], 0.0).then_inc(ev_act, EV_A)

        def a0_scale(n):
            dve.wait_ge(root, n + 1)
            own.step(v.reciprocal(stat[:, 2, n:n + 1], stat[:, 1, n:n + 1]))
            v.scalar_tensor_tensor(out=x_sc[:, n % 2, :], in0=x_in[:, n % NX, :], scalar=stat[:, 2, n:n + 1], in1=g_mix_b[:],
                                   op0=ALU.mult, op1=ALU.mult).then_inc(scaled, 1)

        def a0_lo(n):
            t0, w = tile_cols(n)
            dve.wait_ge(xh_done, n + 1)
            for b in range(2):
                hi, lo = (a[:, 4 * b:4 * b + 4, t0:t0 + w] for a in (xn_hi, xn_lo))
                ins = v.tensor_tensor(lo, split8(ps[:, 4 + 2 * (n % 2) + b, :])[:, :, 0:w], hi.bitcast(F32), ALU.subtract)
            ins.then_inc(xl_done, 1)

        dve.wait_ge(param_in[0], 16)
        a0_scale(0)
        for n in range(1, NT + 1):
            a0_scale(n)
            a0_lo(n - 1)
        a0_lo(NT)
        dve.wait_ge(param_in[1], 16)

        def body_a(j, first, second, end):
            def const(k):
                at_k = j * NCH + k
                return chan_sb[:, at_k:at_k + 1] if isinstance(j, int) else chan_sb[:, bass.ds(at_k, 1)]

            def line(off):
                if isinstance(j, int):
                    return mix[:, off + j, :]
                return mix[:, bass.ds(j + off, 1), :].rearrange("p a t -> p (a t)")

            def taps(lo, hi):
                y = line(0)
                for k in range(lo, hi):
                    src = a_buf[:, k:k + SEQ]
                    if k == 0:
                        ins = v.tensor_scalar(y, src, const(0), const(CB), ALU.mult, ALU.add)
                    else:
                        ins = v.scalar_tensor_tensor(out=y, in0=src, scalar=const(k), in1=y, op0=ALU.mult, op1=ALU.add)
                    if k == TAPS - 1:
                        ins.then_inc(conv_done, 1)
                        dve.wait_ge(conv_done, j + 1)
                    else:
                        own.step(ins)

            for b, (t0, n) in enumerate(BLK):
                dve.wait_ge(ev_act, EV_A * (j + 1) + b + 1)
                dve.wait_ge(proj, 15 * j + 3 + b + 1)
                v.tensor_tensor(a_buf[:, PAD + t0:PAD + t0 + n], bank(UU, b)[:, 0:n], sig[:, t0:t0 + n],
                                ALU.mult).then_inc(ev_dve, 1)
            dve.wait_ge(ev_dve, EV_D * (j + 1) + 3)
            taps(0, first)
            for b, (t0, n) in enumerate(BLK):
                dve.wait_ge(ev_act, EV_A * (j + 1) + 3 + b + 1)
                dve.wait_ge(proj, 15 * j + 9 + b + 1)
                v.tensor_tensor(cv[:, t0:t0 + n], bank(VV, b)[:, 0:n], c_sb[:, t0:t0 + n], ALU.mult).then_inc(ev_dve, 1)
            dve.wait_ge(ev_dve, EV_D * (j + 1) + 6)
            s = line(NJ)
            for k in range(STAPS):
                src = cv[:, META - STAPS + 1 + k:META - STAPS + 1 + k + SEQ]
                if k == 0:
                    own.step(v.tensor_scalar(s, src, const(SW), None, ALU.mult))
                else:
                    own.step(v.scalar_tensor_tensor(out=s, in0=src, scalar=const(SW + k), in1=s, op0=ALU.mult, op1=ALU.add))
            taps(first, second)
            for b, (t0, n) in enumerate(BLK):
                dve.wait_ge(proj, 15 * j + 12 + b + 1)
                skip = META if b == 0 else 0
                o = t0 + skip - META
                if isinstance(j, int):
                    seg = mix[:, NJ + j, o:o + n - skip]
                else:
                    seg = mix[:, bass.ds(j + NJ, 1), o:o + n - skip].rearrange("p a t -> p (a t)")
                v.tensor_tensor(seg, bank(BB, b)[:, skip:n], seg, ALU.mult).then_inc(ev_dve, 1)
            taps(second, end)

        with dve.Fori(0, NJ - 1) as j:
            own.loop(j, TAPS - 1 + STAPS)
            body_a(j, 14, 18, TAPS)
            own.end(NJ - 1)
        body_a(NJ - 1, 14, 17, TAPS - HELP)
        dve.wait_ge(tap_added, HELP - 1)
        v.tensor_tensor(mix[:, NJ - 1, :], mix[:, NJ - 1, :], tap_sum[:], ALU.add).then_inc(conv_done, 1)
        dve.wait_ge(conv_done, NJ)

        def center(h):
            dve.wait_ge(mean_done, h + 1)
            for j in range(NJ):
                v.tensor_tensor(mix[:, j, half(h)], mix[:, j, half(h)], ps[:, 4 + h, :], ALU.subtract).then_inc(cent_done, 1)

        def normalise(q):
            h, part_ = q // 2, slice(256 * (q % 2), 256 * (q % 2) + 256)
            dve.wait_ge(std_done, h + 1)
            own.step(v.reciprocal(rstd[:, h, part_], std[:, h, part_]))
            dve.wait_ge(sq_done, NJ * (h + 1))
            for j in range(NJ):
                ins = v.tensor_tensor(mix[:, j, quarter(q)], mix[:, j, quarter(q)], rstd[:, h, part_], ALU.mult)
            ins.then_inc(nrm_done, 1)
            dve.wait_ge(nrm_done, q + 1)

        center(0)
        center(1)
        normalise(0)
        normalise(1)

        def m_low(t, par):
            dve.wait_ge(mh_done, t + 1)
            v.tensor_tensor(m_lo[:, par], rows(t), m_hi[:, par].bitcast(F32), ALU.subtract).then_inc(ml_done, 1)

        def h_rows(t, par, full):
            dve.wait_ge(xr_full[par], full)
            dve.wait_ge(op_done, t + 1)
            hs = rows(t)
            for b in range(2):
                ins = v.tensor_tensor(hs[:, 4 * b:4 * b + 4, :], split8(ps[:, 2 * par + b, :]),
                                      split8(x_res[:, par, 512 * b:512 * b + 512]), ALU.add)
            ins.then_inc(h_done, 1)

        def hn_rows_of(t, par, stored):
            col = (lambda k: stat[:, k, bass.ds(t + BC, 1)]) if not isinstance(t, int) else (lambda k: stat[:, k, BC + t:BC + t + 1])
            dve.wait_ge(hroot, t + 1)
            if stored is not None:
                dve.wait_ge(hn_out[par], stored)
            own.step(v.reciprocal(col(2), col(1)))
            v.scalar_tensor_tensor(out=hn[:, par, :], in0=rows(t), scalar=col(2), in1=g_ffn_b[:],
                                   op0=ALU.mult, op1=ALU.mult).then_inc(hn_done, 1)

        def logits(t, par):
            dve.wait_ge(rt_done, t + 1)
            o = logit[:, bass.ds(t, 1), :].rearrange("p a n -> p (a n)") if not isinstance(t, int) else logit[:, t, :]
            v.tensor_tensor(o, ps[:, 6 + par, 0:NL], b_rt_b[:], ALU.add).then_inc(lg_done, 1)

        dve.wait_ge(g2_in, 16)
        dve.wait_ge(param_in[3], 16)
        m_low(0, 0)
        m_low(1, 1)
        normalise(2)
        normalise(3)
        h_rows(0, 0, 16)
        hn_rows_of(0, 0, None)
        m_low(2, 0)
        h_rows(1, 1, 16)
        hn_rows_of(1, 1, None)
        m_low(3, 1)
        logits(0, 0)
        h_rows(2, 0, 32)
        hn_rows_of(2, 0, 16)
        with dve.Fori(0, 2) as i:
            own.loop(i, 2)
            for k in range(2):
                m_low(2 * i + 4 + k, k)
                logits(2 * i + 1 + k, 1 - k)
                h_rows(2 * i + 3 + k, 1 - k, 16 * i + 32 + 16 * k)
                hn_rows_of(2 * i + 3 + k, 1 - k, 16 * i + 16 + 16 * k)
            own.end(2)
        logits(5, 1)
        h_rows(7, 1, 64)
        hn_rows_of(7, 1, 48)
        logits(6, 0)
        logits(7, 1)
        dve.wait_ge(lg_done, NT)

        dve.wait_ge(rconsts, 8)
        step = own.step
        lg_g = logit[:, :, 0:NG]
        lg_e = logit[:, :, NG:NL].rearrange("p t (g e) -> p t g e", g=NG)

        def spread(ap, n):
            return ap.unsqueeze(2).broadcast_to([P, ap.shape[1], n])

        def over_tiles(ap, n=NT):
            return ap.unsqueeze(1).broadcast_to([P, n, ap.shape[1]])

        m_g, m_1, m_2, k_m, diff, q_e, g_sum, g_top, den, r_den = (vec[:, k, :] for k in range(10))
        step(v.tensor_reduce(m_g, lg_g, AX.X, ALU.max))
        v.tensor_tensor(g_sh[:], lg_g, spread(m_g, NG), ALU.subtract).then_inc(exp_in, 1)

        def first_max(src, top, n, keybuf, onehot):
            step(v.tensor_tensor(keybuf, src, spread(top, n), ALU.is_equal))
            step(v.tensor_tensor(keybuf, keybuf, over_tiles(rev[:, NEG - n:NEG]), ALU.mult))
            step(v.tensor_reduce(k_m, keybuf, AX.X, ALU.max))
            step(v.tensor_tensor(onehot, keybuf, spread(k_m, n), ALU.is_equal))

        first_max(lg_g, m_g, NG, g_key[:], g_one[:])
        one4 = g_one[:].unsqueeze(3).broadcast_to([P, NT, NG, NEG])
        step(v.tensor_tensor(a1[:], lg_e, one4, ALU.mult))
        step(v.tensor_reduce(sel[:], a1[:].rearrange("p t g e -> p t e g"), AX.X, ALU.add))
        step(v.tensor_reduce(m_1, sel[:], AX.X, ALU.max))
        first_max(sel[:], m_1, NEG, key[:], o1[:])
        step(v.scalar_tensor_tensor(out=sel2[:], in0=o1[:], scalar=-3.0e38, in1=sel[:], op0=ALU.mult, op1=ALU.add))
        step(v.tensor_reduce(m_2, sel2[:], AX.X, ALU.max))
        v.tensor_tensor(diff, m_2, m_1, ALU.subtract).then_inc(exp_in, 1)
        first_max(sel2[:], m_2, NEG, key[:], o2[:])
        for a, o in ((a1, o1), (a2, o2)):
            step(v.tensor_tensor(a[:], o[:].unsqueeze(2).broadcast_to([P, NT, NG, NEG]), one4, ALU.mult))
        flat1, flat2 = (a[:].rearrange("p t g e -> p t (g e)") for a in (a1, a2))
        v.tensor_tensor(a12[:], flat1, flat2, ALU.add).then_inc(a_ready, 1)
        dve.wait_ge(exp_out, 2)
        step(v.tensor_reduce(g_sum, g_ex[:], AX.X, ALU.add))
        step(v.reciprocal(g_top, g_sum))
        step(v.tensor_scalar(den, q_e, 1.0, None, ALU.add))
        step(v.reciprocal(r_den, den))
        step(v.tensor_tensor(wk[:, 0, :], g_top, r_den, ALU.mult))
        step(v.tensor_tensor(wk[:, 1, :], wk[:, 0, :], q_e, ALU.mult))
        step(v.tensor_copy(wk_hi[:], wk[:]))
        step(v.tensor_tensor(wk_lo[:], wk[:], wk_hi[:].bitcast(F32), ALU.subtract))
        for h in range(2):
            dve.wait_ge(hn_out[h], 16 * NT // 2)
        dve.wait_ge(ranks, 1)
        step(v.tensor_reduce(count[:], ps[:, 6, 0:NT * NE].rearrange("p (t e) -> p e t", e=NE), AX.X, ALU.add))
        step(v.tensor_tensor(more[:], over_tiles(count[:], 7), thr[:], ALU.is_gt))
        step(v.tensor_reduce(nblk[:], more[:].rearrange("p b e -> p e b"), AX.X, ALU.add))
        step(v.tensor_scalar(nblk[:], nblk[:], 1.0, None, ALU.add))
        step(v.tensor_tensor_scan(s_end[:], ones[:, 0:NE], nblk[:], 0.0, ALU.mult, ALU.add))
        step(v.tensor_tensor(s_beg[:], s_end[:], nblk[:], ALU.subtract))
        dve.wait_ge(ranks, 2)
        step(v.scalar_tensor_tensor(out=dest[:], in0=over_tiles(s_beg[:]), scalar=float(P),
                                    in1=ps[:, 7, 0:NT * NE].rearrange("p (t e) -> p t e", e=NE), op0=ALU.mult, op1=ALU.add))
        for k, a in enumerate((flat1, flat2)):
            step(v.tensor_tensor(prod[:], dest[:], a, ALU.mult))
            step(v.tensor_reduce(dd[:, k, :], prod[:], AX.X, ALU.add))
        step(v.tensor_copy(dd_i[:], dd[:]))
        step(v.tensor_scalar(sl_i[:], dd_i[:], 7, None, ALU.arith_shift_right))
        step(v.tensor_scalar(ro_i[:], dd_i[:], P - 1, None, ALU.bitwise_and))
        step(v.tensor_copy(sl_f[:], sl_i[:]))
        step(v.tensor_copy(ro_f[:], ro_i[:]))
        for k in range(2):
            a = slice(k * NT, k * NT + NT)
            v.tensor_tensor(one_r[:, a, :], over_tiles(iota_r[:]), spread(ro_f[:, k, :], P),
                            ALU.is_equal).then_inc(inv_in, 1)
            v.tensor_tensor(one_s[:, a, :], over_tiles(iota_s[:]), spread(sl_f[:, k, :], SLOTS),
                            ALU.is_equal).then_inc(inv_in, 1)
            dve.wait_ge(inv_in, 5 * k + 2)
            for i, value in enumerate((asg_id[:], wk_hi[:].bitcast(F32), wk_lo[:].bitcast(F32))):
                v.tensor_tensor(val_s[:, a, i, :], one_s[:, a, :], spread(value[:, k, :], SLOTS),
                                ALU.mult).then_inc(inv_in, 1)
        step(v.tensor_scalar(junk[:], s_end[:], part[:], 0.0, ALU.is_le, ALU.add, accum_out=tab[:, 0:1]))
        v.tensor_scalar(tab[:, 0:1], tab[:, 0:1], float(NE - 1), None, ALU.min).then_inc(tab_in, 1)
        step(v.tensor_scalar(expert_last[:], s_end[0:1, :], -1.0, None, ALU.add))
        dve.wait_ge(inv_out, 1)
        step(v.tensor_scalar(sidx[:], ps[:, 6, 0:SLOTS], float(OOB), None, ALU.add))
        v.tensor_scalar(gidx[:], sidx[:], OOB + SEQ - 1, None, ALU.bitwise_and).then_inc(gidx_ready, 1)
        v.tensor_copy(id_inv[:], ps[:, 6, 0:SLOTS]).then_inc(tab_in, 1)
        step(v.tensor_copy(w_inv[:], ps[:, 6, SLOTS:2 * SLOTS]))
        step(v.tensor_tensor(wgt[:], ps[:, 6, 2 * SLOTS:3 * SLOTS], w_inv[:], ALU.add))
        dve.wait_ge(tab_out, 1)
        v.tensor_scalar(slot_big[:], ps[0:1, 5, P:P + SLOTS], 0.0, None, ALU.is_lt)
        step(v.tensor_copy(slot_expert[:], ps[0:1, 5, 0:SLOTS]))
        v.tensor_scalar(slot_even[:], slot_expert[:], 1, 1, ALU.bitwise_and, ALU.bitwise_xor).then_inc(tables, 1)

        def low(n, place, c, even, inc=1):
            dve.wait_ge(part_h, n + 1)
            r_ = ring[place % RING]
            v.tensor_tensor(r_[:, 1, :], raw_chunk(even, c), r_[:, 0, :].bitcast(F32), ALU.subtract).then_inc(part_l, inc)

        def xt_low(count):
            dve.wait_ge(xt_h, count)
            for b in range(2):
                ins = v.tensor_tensor(xt_lo[:, 4 * b:4 * b + 4, :], split8(ps[:, 4 + b, :]),
                                      xt_hi[:, 4 * b:4 * b + 4, :].bitcast(F32), ALU.subtract)
            ins.then_inc(xt_l, 1)

        def ht_low(s):
            dve.wait_ge(ht_h, s + 1)
            v.tensor_tensor(ht_lo[:], split8(ps[:, 6, :]), ht_hi[:].bitcast(F32), ALU.subtract).then_inc(ht_l, 1)

        dve.wait_ge(tables, 1)
        last = dve.value_load(expert_last[0:1, NE - 1:NE], min_val=NE - 1, max_val=MAX_LAST)

        def even_of(g):
            return dve.value_load(slot_even[0:1, bass.ds(g, 1)], min_val=0, max_val=1)

        def hidden(g):
            dve.wait_ge(sil_done, g + 1)
            v.tensor_tensor(hid[:], ps[:, 1, :], sil[:], ALU.mult).then_inc(hid_done, 1)

        low(0, 0, 0, 1)
        low(1, 1, 1, 1)
        xt_low(1)
        for c in range(2, GUC):
            low(c, c, c, 1, 1 + DNC if c == GUC - 1 else 1)
        hidden(0)
        xt_low(2)
        with dve.Fori(0, MAX_LAST + 1) as s:
            with dve.If(s < last):
                now = even_of(s + 1)
                n = s * NC + GUC
                for c in range(GUC):
                    if c == 6:
                        ht_low(s)
                    low(n + c, 2 + c, c, now)
                before = even_of(s)
                for c in range(GUC, NC):
                    low(n + c, 2 + c, c, before)
                hidden(s + 1)
                xt_low(s + 3)
            with dve.Else():
                with dve.If(s < last + 1):
                    for c in range(DNC):
                        low(s * NC + GUC + c, 2 + c, GUC + c, 0)
                    ht_low(s)

        def f_out(t):
            dve.wait_ge(froot, t + 1)
            step(v.reciprocal(stat[:, 2, FC + t:FC + t + 1], stat[:, 1, FC + t:FC + t + 1]))
            v.scalar_tensor_tensor(out=ys[:, t, 1, :], in0=ys[:, t, 0, :], scalar=stat[:, 2, FC + t:FC + t + 1],
                                   in1=g_fin_b[:], op0=ALU.mult, op1=ALU.mult).then_inc(o_done, 1)

        dve.wait_ge(g3_in, 16)
        for t in range(NT):
            dve.wait_ge(ys_full[t], 32)
            step(v.tensor_tensor(split8(ys[:, t, 0, :]), rows(t), split8(ys[:, t, 0, :]), ALU.add))
            v.tensor_tensor(ys[:, t, 0, :], ys[:, t, 0, :], ys[:, t, 1, :], ALU.add).then_inc(z_done, 1)
            if t >= 1:
                dve.wait_ge(z_done, t + 1)
                f_out(t - 1)
        f_out(NT - 1)

    @block.tensor
    def _(pe):
        mm = nc.tensor.matmul

        def three(o, s_hi, s_lo, m_hi_, m_lo_, start, stop):
            mm(o, s_hi, m_hi_, start=start, stop=False)
            mm(o, s_hi, m_lo_, start=False, stop=False)
            return mm(o, s_lo, m_hi_, start=False, stop=stop)

        pe.wait_ge(consts, 2)

        def turn(src, banks, step_k):
            for k in range(KD):
                ins = nc.tensor.transpose(ps[:, banks + k // 4, (k % 4) * P:(k % 4 + 1) * P],
                                          src[:, k:D:KD] if step_k else src[:, k * P:(k + 1) * P], ident[:])
            return ins

        def a0_turn(n, half):
            pe.wait_ge(scaled, n + 1)
            if not isinstance(n, int) or n >= 2:
                pe.wait_ge(xl_done, n - 1)
            turn(x_sc[:, half, :], 4 + 2 * half, False).then_inc(turned, 1)

        def taken(j, n):
            q, b = n % 15 // 3, n % 3
            turn_ = j + 1 if n >= 0 else j
            if q in (GL, CC):
                pe.wait_ge(ev_act, EV_A * turn_ + (3 if q == CC else 0) + b + 1)
            else:
                pe.wait_ge(ev_dve, EV_D * turn_ + {UU: 0, VV: 3, BB: 6}[q] + b + 1)

        def project(j, q, b, ks=range(KD)):
            t0, n = BLK[b]
            if b == 0 and ks[0] == 0:
                pe.wait_ge(wi_l, ROLES * j + q + 1)
            i = 3 * q + b
            if i >= 8:
                taken(j, i - 8)
            elif not isinstance(j, int) or j:
                taken(j, (7 if i == 7 else i + 8) - 15)
            for k in ks:
                ins = three(bank(q, b)[:, 0:n], wi_hi[:, q, k * P:(k + 1) * P], wi_lo[:, q, k * P:(k + 1) * P],
                            xn_hi[:, k, t0:t0 + n], xn_lo[:, k, t0:t0 + n], k == 0, k == KD - 1)
            if ks[-1] == KD - 1:
                ins.then_inc(proj, 1)

        EARLY = {5: (0, range(0, 4)), 6: (0, range(4, 8)), 7: (1, range(0, 4)), 8: (1, range(4, 8))}

        for n in range(NT + 1):
            a0_turn(n, n % 2)
            if n in EARLY:
                b, ks = EARLY[n]
                pe.wait_ge(xl_done, -(-(BLK[b][0] + BLK[b][1] - META) // P) + 1)
                project(0, GL, b, ks)
        pe.wait_ge(xl_done, NT + 1)
        project(0, GL, 2)
        with pe.Fori(0, NJ - 1) as j:
            for q in (UU, CC, VV, BB):
                for b in range(3):
                    project(j, q, b)
            for b in range(3):
                project(j + 1, GL, b)
        for q in (UU, CC, VV, BB):
            for b in range(3):
                project(NJ - 1, q, b)

        pe.wait_ge(ev_dve, EV_D * NJ + 9)
        for j in range(NJ):
            pe.wait_ge(conv_done, j + 1)
            for h in range(2):
                ins = mm(ps[:, 4 + h, :], ones_cw[:], mix[:, j, half(h)], start=j == 0, stop=j == NJ - 1)
                if j == NJ - 1:
                    ins.then_inc(mean_done, 1)
        for h in range(2):
            for j in range(NJ):
                pe.wait_ge(sq_done, h * NJ + j + 1)
                ins = mm(ps[:, 6 + h, :], ones_cw[:], sq[:, h, j, :], start=j == 0, stop=j == NJ - 1)
            ins.then_inc(var_done, 1)

        def out_proj(t, par):
            pe.wait_ge(ml_done, t + 1)
            if not isinstance(t, int) or t >= 2:
                pe.wait_ge(h_done, t - 1)
            for b in range(2):
                for k in range(KD):
                    ins = three(ps[:, 2 * par + b, :], m_hi[:, par, k, :], m_lo[:, par, k, :],
                                wo_hi[:, k, 512 * b:512 * b + 512], wo_lo[:, k, 512 * b:512 * b + 512], k == 0, k == KD - 1)
            ins.then_inc(op_done, 1)

        def turn_h(t, par):
            pe.wait_ge(hn_done, t + 1)
            if not isinstance(t, int) or t >= 1:
                pe.wait_ge(hnt_done, t)
            turn(hn[:, par, :], 4, False).then_inc(hturned, 1)

        def router(t, par):
            pe.wait_ge(hnt_done, t + 1)
            for k in range(KD):
                ins = mm(ps[:, 6 + par, 0:NL], hn_t[:, k, :], w_rt_sb[:, k, :], start=k == 0, stop=k == KD - 1)
            ins.then_inc(rt_done, 1)

        pe.wait_ge(wo_l, KD)
        pe.wait_ge(param_in[2], 16)
        out_proj(0, 0)
        out_proj(1, 1)
        turn_h(0, 0)
        with pe.Fori(0, 3) as i:
            for k in range(2):
                out_proj(2 * i + 2 + k, k)
                router(2 * i + k, k)
                turn_h(2 * i + 1 + k, 1 - k)
        router(6, 0)
        turn_h(7, 1)
        router(7, 1)

        pe.wait_ge(rconsts, 8)
        pe.wait_ge(a_ready, 1)
        mm(ps[:, 6, 0:NT * NE], ones_r[:], a12[:].rearrange("p t e -> p (t e)"), start=True, stop=True).then_inc(ranks, 1)
        mm(ps[:, 7, 0:NT * NE], tri_r[:], a12[:].rearrange("p t e -> p (t e)"), start=True, stop=False)
        for t in range(NT - 1):
            ins = mm(ps[:, 7, (t + 1) * NE:NT * NE].rearrange("p (t e) -> p t e", e=NE), ones_r[:],
                     a12[:, t, :].unsqueeze(1).broadcast_to([P, NT - 1 - t, NE]), start=False, stop=t == NT - 2)
        ins.then_inc(ranks, 1)
        for a in range(2 * NT):
            if a % NT == 0:
                pe.wait_ge(inv_in, 5 * (a // NT) + 5)
            ins = mm(ps[:, 6, 0:3 * SLOTS], one_r[:, a, :], val_s[:, a].rearrange("p k s -> p (k s)"),
                     start=a == 0, stop=a == 2 * NT - 1)
        ins.then_inc(inv_out, 1)
        pe.wait_ge(tab_in, 1)
        mm(ps[0:1, 5, 0:P], tab[:], ident[:], start=True, stop=True)
        pe.wait_ge(tab_in, 2)
        mm(ps[0:1, 5, P:P + SLOTS], ident[:, HALF:HALF + 1], id_inv[:], start=True, stop=True).then_inc(tab_out, 1)

        def turn_x(count):
            pe.wait_ge(gathered, count * 16)
            turn(x_g[:], 4, True).then_inc(xt_done, 1)

        def turn_hid(s):
            pe.wait_ge(hid_done, s + 1)
            for k in range(KF):
                ins = nc.tensor.transpose(ps[:, 6, k * P:(k + 1) * P], hid[:, k:F:KF], ident[:])
            ins.then_inc(ht_done, 1)

        def gate_up(g, place, middle):
            pe.wait_ge(xt_l, g + 1)
            if middle is not None:
                pe.wait_ge(hid_done, middle + 1)
            for c in range(GUC):
                pe.wait_ge(part_l, g * NC + c + 1)
                r_ = ring[(place + c) % RING]
                for kk in range(2):
                    k = 2 * (c // 2) + kk
                    cols = slice(512 * kk, 512 * kk + 512)
                    ins = three(ps[:, c % 2, :], xt_hi[:, k, :], xt_lo[:, k, :], r_[:, 0, cols], r_[:, 1, cols],
                                k == 0, k == KD - 1)
                ins.then_inc(used, 1)
                if c == 3 and middle is not None:
                    turn_hid(middle)

        def down(s, count, place):
            pe.wait_ge(ht_l, s + 1)
            for c in range(DNC):
                pe.wait_ge(part_l, count + c + 1)
                r_ = ring[(place + c) % RING]
                for n in range(2):
                    cols = slice(512 * n, 512 * n + 512)
                    ins = three(ps[:, 2 + n, :], ht_hi[:, c, :], ht_lo[:, c, :], r_[:, 0, cols], r_[:, 1, cols],
                                c == 0, c == DNC - 1)
                ins.then_inc(used, 1)

        pe.wait_ge(tables, 1)
        last = pe.value_load(expert_last[0:1, NE - 1:NE], min_val=NE - 1, max_val=MAX_LAST)
        turn_x(1)
        gate_up(0, 0, None)
        turn_x(2)
        with pe.Fori(0, MAX_LAST + 1) as s:
            with pe.If(s < last):
                gate_up(s + 1, 2, s)
                pe.wait_ge(xt_l, s + 2)
                turn_x(s + 3)
                down(s, s * NC + NC + GUC, 2 + GUC)
            with pe.Else():
                with pe.If(s < last + 1):
                    turn_hid(s)
                    down(s, s * NC + NC, 2)

    block_cm.__exit__(None, None, None)


def kernel(x, meta_tokens, norm_mix_g, w_in, conf_dw_w, conf_dw_b, conf_ln_g, conf_ln_b, sc_conv_w, w_out, norm_ffn_g,
           w_router_group, b_router_group, w_router_expert, b_router_expert, w_exp_gate, w_exp_up, w_exp_down,
           final_norm_g):
    import numpy as np
    import concourse.bacc as bacc
    from concourse.bass_utils import run_bass_kernel_spmd

    a = {k: np.ascontiguousarray(v) for k, v in dict(
        x=x, meta=meta_tokens, w_in=w_in, w_out=w_out, g_mix=norm_mix_g, g_ffn=norm_ffn_g, g_fin=final_norm_g,
        cw=conf_dw_w, cb=conf_dw_b, lg=conf_ln_g, lb=conf_ln_b, sw=sc_conv_w, rg=w_router_group, bg=b_router_group,
        re=w_router_expert, be=b_router_expert, wg=w_exp_gate, wu=w_exp_up, wd=w_exp_down).items()}
    parts = a["w_in"][0].reshape(KD, P, 5, NJ, P)[:, :, [1, 0, 3, 4, 2]]
    w_in_l = np.ascontiguousarray(parts.transpose(3, 2, 1, 0, 4)).reshape(NJ * ROLES, P, KD * P)
    chan = np.concatenate([a["cw"][0], a["cb"], a["lg"], a["lb"], a["sw"][0]], axis=0)
    chan = np.ascontiguousarray(chan.reshape(NCH, NJ, P).transpose(2, 1, 0)).reshape(P, NJ * NCH)
    arrays = {
        "x": a["x"][0], "meta": a["meta"], "w_in": w_in_l, "chan": chan, "g_mix": a["g_mix"][0], "w_out": a["w_out"][0],
        "g_ffn": a["g_ffn"][0],
        "w_rt": np.ascontiguousarray(np.concatenate([a["rg"][0], a["re"][0]], axis=1)),
        "b_rt": np.ascontiguousarray(np.concatenate([a["bg"][0], a["be"][0]])),
        "w_gate": a["wg"][0], "w_up": a["wu"][0], "w_down": a["wd"][0], "g_fin": a["g_fin"],
    }
    nc = bacc.Bacc("TRN2", target_bir_lowering=False, num_devices=1)
    args = [nc.dram_tensor(f"in_{k}", v.shape, mybir.dt.from_np(v.dtype), kind="ExternalInput").ap()
            for k, v in arrays.items()]
    args.append(nc.dram_tensor("out_0", (SEQ, D), F32, kind="ExternalOutput").ap())
    trunk(nc, *args)
    r = run_bass_kernel_spmd(nc, [{f"in_{k}": v for k, v in arrays.items()}], core_ids=[0])
    return r.results[0]["out_0"].reshape(1, SEQ, D)
```
